# Optimizing a Trainium2 kernel written in Bass

```python
import jax, jax.numpy as jnp
from jax import lax
import numpy as np

D_MODEL = 1024
BATCH = 1
SEQ = 1024
DEPTH = 1

HEAD_DIM = 64
D_MIX = D_MODEL
D_ATTN = D_MIX // 2
D_POOL = D_MIX // 4
D_CONV = D_MIX // 4
N_ATTN_HEADS = D_ATTN // HEAD_DIM
POOL_WINDOWS = (2, 4, 8, 16)
N_POOL_GROUPS = len(POOL_WINDOWS)
POOL_GROUP_DIM = D_POOL // N_POOL_GROUPS
N_CONV_HEADS = D_CONV // HEAD_DIM
CONV_WIDTH = 3
D_FF = 2816
Q_BLOCK = 128
RMS_EPS = 1e-6
IN_SPLITS = (D_ATTN, D_ATTN, D_ATTN, N_ATTN_HEADS, D_POOL, D_CONV, D_CONV, D_CONV)
D_IN = sum(IN_SPLITS)

kernel_name = "hymba_style_fox_pool_shortconv_macaron"

def _rmsnorm(x, g):
    x32 = x.astype(jnp.float32)
    y = x32 * lax.rsqrt(jnp.mean(x32 * x32, axis=-1, keepdims=True) + RMS_EPS)
    return (y * g.astype(jnp.float32)).astype(x.dtype)

def _swiglu(h, w_in, w_out):
    gate, up = jnp.split(h @ w_in, 2, axis=-1)
    return (jax.nn.silu(gate) * up) @ w_out

def _fox_attention(q, k, v, f_logit, b_forget):
    b, s, _ = q.shape
    qh = q.reshape(b, s, N_ATTN_HEADS, HEAD_DIM).transpose(0, 2, 1, 3)
    kh = k.reshape(b, s, N_ATTN_HEADS, HEAD_DIM).transpose(0, 2, 1, 3)
    vh = v.reshape(b, s, N_ATTN_HEADS, HEAD_DIM).transpose(0, 2, 1, 3)
    log_f = jax.nn.log_sigmoid(f_logit.astype(jnp.float32) + b_forget.astype(jnp.float32))
    dcum = lax.cumsum(log_f, axis=1).transpose(0, 2, 1)
    scale = HEAD_DIM ** -0.5
    outs = []
    for i in range(s // Q_BLOCK):
        q0 = i * Q_BLOCK
        end = q0 + Q_BLOCK
        sc = jnp.einsum('bhqd,bhkd->bhqk', qh[:, :, q0:end], kh[:, :, :end],
                        preferred_element_type=jnp.float32) * scale
        sc = sc + dcum[:, :, q0:end, None] - dcum[:, :, None, :end]
        mask = jnp.arange(end)[None, :] <= (q0 + jnp.arange(Q_BLOCK))[:, None]
        sc = jnp.where(mask, sc, -jnp.inf)
        p = jax.nn.softmax(sc, axis=-1)
        outs.append(jnp.einsum('bhqk,bhkd->bhqd', p.astype(vh.dtype), vh[:, :, :end]))
    o = jnp.concatenate(outs, axis=2)
    return o.transpose(0, 2, 1, 3).reshape(b, s, D_ATTN)

def _multiscale_pool(u, w_pool, pool_scale):
    b, s, _ = u.shape
    groups = jnp.split(u, N_POOL_GROUPS, axis=-1)
    pos = jnp.arange(s)
    outs = []
    for gi, w in enumerate(POOL_WINDOWS):
        ug = groups[gi]
        cs = lax.cumsum(ug.astype(jnp.float32), axis=1)
        cs_pad = jnp.pad(cs, ((0, 0), (w, 0), (0, 0)))
        win_sum = cs - cs_pad[:, :s]
        count = jnp.minimum(pos + 1, w).astype(jnp.float32)[None, :, None]
        pooled = (win_sum / count).astype(ug.dtype) - ug
        outs.append(jnp.einsum('bsc,cd->bsd', pooled, w_pool[gi]))
    return jnp.concatenate(outs, axis=-1) * pool_scale

def _short_conv(b_gate, c_gate, h, conv_w):
    u = c_gate * h
    rhs = conv_w.reshape(CONV_WIDTH, 1, D_CONV).astype(u.dtype)
    y = lax.conv_general_dilated(u, rhs, window_strides=(1,), padding=((CONV_WIDTH - 1, 0),),
                                 dimension_numbers=('NWC', 'WIO', 'NWC'),
                                 feature_group_count=D_CONV)
    return b_gate * y

def _hybrid_mixer(xn, w_in, b_forget, w_pool, pool_scale, conv_w, w_out):
    proj = xn @ w_in
    idx = list(np.cumsum(IN_SPLITS)[:-1])
    q, k, v, f_logit, pool_in, cb, cc, ch = jnp.split(proj, idx, axis=-1)
    y_attn = _fox_attention(q, k, v, f_logit, b_forget)
    y_pool = _multiscale_pool(pool_in, w_pool, pool_scale)
    y_conv = _short_conv(cb, cc, ch, conv_w)
    return jnp.concatenate([y_attn, y_pool, y_conv], axis=-1) @ w_out

def setup_inputs(seed: int = 0) -> dict:
    key = jax.random.key(seed)
    ks = jax.random.split(key, 16)
    f32 = jnp.float32

    def nrm(k, shape, fan_in):
        return jax.random.normal(k, shape, f32) * (fan_in ** -0.5)

    def gain(k, shape):
        return 1.0 + 0.1 * jax.random.normal(k, shape, f32)

    return {
        "x": jax.random.normal(ks[0], (BATCH, SEQ, D_MODEL), f32),
        "norm_ffn1": gain(ks[1], (DEPTH, D_MODEL)),
        "w_ffn1_in": nrm(ks[2], (DEPTH, D_MODEL, 2 * D_FF), D_MODEL),
        "w_ffn1_out": nrm(ks[3], (DEPTH, D_FF, D_MODEL), D_FF),
        "norm_mix": gain(ks[4], (DEPTH, D_MODEL)),
        "w_mix_in": nrm(ks[5], (DEPTH, D_MODEL, D_IN), D_MODEL),
        "b_forget": 3.0 + 0.5 * jax.random.normal(ks[6], (DEPTH, N_ATTN_HEADS), f32),
        "w_pool": nrm(ks[7], (DEPTH, N_POOL_GROUPS, POOL_GROUP_DIM, POOL_GROUP_DIM), POOL_GROUP_DIM),
        "pool_scale": gain(ks[8], (DEPTH, D_POOL)),
        "conv_w": nrm(ks[9], (DEPTH, CONV_WIDTH, D_CONV), CONV_WIDTH),
        "w_mix_out": nrm(ks[10], (DEPTH, D_MIX, D_MODEL), D_MIX),
        "norm_ffn2": gain(ks[11], (DEPTH, D_MODEL)),
        "w_ffn2_in": nrm(ks[12], (DEPTH, D_MODEL, 2 * D_FF), D_MODEL),
        "w_ffn2_out": nrm(ks[13], (DEPTH, D_FF, D_MODEL), D_FF),
        "norm_final": gain(ks[14], (D_MODEL,)),
    }

def reference(x, norm_ffn1, w_ffn1_in, w_ffn1_out, norm_mix, w_mix_in, b_forget, w_pool,
              pool_scale, conv_w, w_mix_out, norm_ffn2, w_ffn2_in, w_ffn2_out, norm_final):
    for l in range(DEPTH):
        x = x + 0.5 * _swiglu(_rmsnorm(x, norm_ffn1[l]), w_ffn1_in[l], w_ffn1_out[l])
        x = x + _hybrid_mixer(_rmsnorm(x, norm_mix[l]), w_mix_in[l], b_forget[l], w_pool[l],
                              pool_scale[l], conv_w[l], w_mix_out[l])
        x = x + 0.5 * _swiglu(_rmsnorm(x, norm_ffn2[l]), w_ffn2_in[l], w_ffn2_out[l])
    return _rmsnorm(x, norm_final)


_drawn_inputs = setup_inputs


def setup_inputs(seed=0):
    import zlib

    import numpy as np

    out = dict(_drawn_inputs(seed))
    spreads = {}
    factors = {}
    for name, (base, spread) in spreads.items():
        noise = np.random.default_rng([zlib.crc32(name.encode()), seed]).standard_normal(out[name].shape)
        drawn = base * np.exp(spread * noise) if base else spread * noise
        out[name] = __import__('jax').numpy.asarray(drawn.astype(out[name].dtype))
    for name, factor in factors.items():
        out[name] = (out[name] * factor).astype(out[name].dtype)
    return out
```

```python
from contextlib import ExitStack

import concourse.bass as bass
from concourse import mybir

F32 = mybir.dt.float32
F32R = mybir.dt.float32r
ALU = mybir.AluOpType
ACT = mybir.ActivationFunctionType
AX = mybir.AxisListType

P = 128
D = 1024
T = 1024
KD = D // P
NT = T // P
BANK = 512
F = 2816
PAIR = 2 * P
GROUPS = F // PAIR
TURNS = (GROUPS - 1) // 2
HEADS = 8
HD = 64
D_ATTN = HEADS * HD
COL_Q, COL_K, COL_V = 0, D_ATTN, 2 * D_ATTN
COL_F = 3 * D_ATTN
COL_POOL = COL_F + HEADS
COL_CB = COL_POOL + PAIR
COL_CC = COL_CB + PAIR
COL_CH = COL_CC + PAIR
WINDOWS = (2, 4, 8, 16)
WMAX = WINDOWS[-1]
TAPS = 3
EPS = 1e-6
SCALE = HD ** -0.5
MASKED = -1.0e30
HI, LO = 0, 1
PASSES = ((LO, HI), (HI, LO), (HI, HI))

V_NORM1, V_MIX, V_NORM2, V_FINAL = 0, KD, 2 * KD, 3 * KD
V_CONV = 4 * KD
V_PSCALE = V_CONV + 2 * TAPS
V_BFORGET = V_PSCALE + 2
V_COUNT = V_BFORGET + 1
V_ALL = V_COUNT + 2 * WMAX

(N_POOL, N_CC, N_CH, N_CB, N_OUT_POOL, N_V0, N_V1, N_OUT_CONV,
 N_Q0, N_Q1, N_K0, N_K1) = range(3 * GROUPS, 3 * GROUPS + 12)
N_FFN = (0, N_K1 + 1)
ATTN_SLOT = N_FFN[1] % 2

X_FFN1 = KD
X_MIX = X_FFN1 + KD * GROUPS
X_ATTN = X_MIX + 2 * KD
X_FFN2 = X_ATTN + 2 * 2 * KD
X_END = X_FFN2 + KD * GROUPS
X_BASE = (X_FFN1, X_FFN2)

TURN_HEADS = 4
STEPS = TURN_HEADS * NT
QG = 2 * P
GROUPS_PER_HEAD = T // QG
TURN_GROUPS = TURN_HEADS * GROUPS_PER_HEAD

KB = 1024
SBUF_START, SBUF_END = 16512, 229344


def gate_pair(g):
    return 3 * g - 1 if g else 0


def down_pair(g):
    return 3 * g + 4 if g < GROUPS - 1 else 3 * GROUPS - 1


def trunk(nc, x, w1_in, w1_out, wm_in, wm_out, w_pool, w2_in, w2_out, vectors, out):
    with ExitStack() as ctx:
        def sem(name):
            return ctx.enter_context(nc.semaphore(name))

        place = [SBUF_START]

        def at(offset, name, shape, dt):
            size = 4
            for n in shape[1:]:
                size *= n
            assert offset + size <= SBUF_END, (name, offset + size - SBUF_END)
            return nc.alloc_sbuf_tensor_at(name, shape, dt, offset=offset)

        def keep(name, shape, dt):
            size = 4
            for n in shape[1:]:
                size *= n
            offset = place[0]
            place[0] += (size + 31) // 32 * 32
            return at(offset, name, shape, dt)

        xt = keep("xt", [P, KD, T], F32)
        r_rows = keep("r_rows", [P, T], F32)
        raw = keep("raw", [P, 2, KD * PAIR], F32)
        vec = keep("vec", [P, V_ALL], F32)
        ident = keep("ident", [P, P], F32)
        ident_r = keep("ident_r", [P, P], F32R)
        causal_r = keep("causal_r", [P, P], F32R)
        tri = keep("tri", [P, P], F32)
        ones2 = keep("ones2", [P, 2], F32)
        head_mask = keep("head_mask", [P, HEADS], F32)
        ms = keep("ms", [P, NT], F32)
        root = keep("root", [P, NT], F32)
        newton = keep("newton", [P, NT], F32)
        r_col = keep("r_col", [P, NT], F32)
        stat = keep("stat", [P, 4, 2], F32)
        head_col = keep("head_col", [P, 1], F32)
        wf_raw = keep("wf_raw", [P, KD, HEADS], F32)

        a0 = place[0]
        xg = at(a0, "xg", [P, 2, KD, T], F32R)
        w_a = at(a0 + 64 * KB, "w_a", [P, 2, KD, PAIR], F32R)
        w_b = at(a0 + 80 * KB, "w_b", [P, 2, KD, PAIR], F32R)
        w_o = at(a0 + 96 * KB, "w_o", [P, 2, 2, D], F32R)
        hid0 = at(a0 + 112 * KB, "hid0", [P, 2, 2, T], F32R)
        hid1 = at(a0 + 128 * KB, "hid1", [P, 2, 2, T], F32R)
        tmp = at(a0 + 144 * KB, "tmp", [P, 2, T], F32)
        hid = (hid0, hid1)
        x_in = at(a0 + 96 * KB, "x_in", [P, NT, D], F32)
        mix = at(a0 + 128 * KB, "mix", [P, 5 * T + 32], F32)
        wp_raw = at(a0 + 149 * KB, "wp_raw", [P, 2, P], F32)
        wp_r = at(a0 + 150 * KB, "wp_r", [P, 2, 2, P], F32R)
        v_plain = at(a0 + 128 * KB, "v_plain", [P, NT, D_ATTN], F32)
        q_plain = at(a0 + 96 * KB, "q_plain", [P, 4, T], F32)
        k_plain = at(a0 + 112 * KB, "k_plain", [P, 4, T], F32)
        q_st = at(a0 + 0 * KB, "q_st", [P, 2, T], F32R)
        k_hi = at(a0 + 8 * KB, "k_hi", [P, 2, T], F32R)
        k_lo = at(a0 + 16 * KB, "k_lo", [P, 2, T], F32R)
        v_st = at(a0 + 24 * KB, "v_st", [P, 2, NT, 2 * HD], F32R)
        decay_k = at(a0 + 32 * KB, "decay_k", [P, T], F32R)
        decay_h = at(a0 + 36 * KB, "decay_h", [P, T], F32R)
        decay_q = at(a0 + 40 * KB, "decay_q", [P, T], F32R)
        y_f = at(a0 + 44 * KB, "y_f", [P, T], F32)
        pt = at(a0 + 48 * KB, "pt", [P, 2, NT, QG], F32R)
        a_wo = at(a0 + 64 * KB, "a_wo", [P, 2, 2, D], F32R)
        a_y = at(a0 + 80 * KB, "a_y", [P, 2, 2, T], F32R)
        prob = tmp
        x_gain = at(a0, "x_gain", [P, KD, T], F32)
        x_out = at(a0 + 32 * KB, "x_out", [P, NT, D], F32)

        wf = w_a[:, HI, :, 0:P]

        def row(s, quadrant):
            return tmp[32 * quadrant:32 * quadrant + HEADS, s, :]

        pool_u = mix[:, 0:T]
        pool_a = mix[:, T:2 * T + WMAX]
        pool_b = mix[:, 2 * T + WMAX:3 * T + 2 * WMAX]
        conv_cc = mix[:, 3 * T + 32:5 * T + 32].rearrange("p (c t) -> p c t", c=2)
        conv_u = mix[:, 0:2 * (T + 2)].rearrange("p (c t) -> p c t", c=2)
        conv_b = mix[:, 2 * T + 16:3 * T + 16]

        ps = ctx.enter_context(nc.psum_tensor("ps", [P, 8, BANK], F32))

        def unit(slot):
            return ps[:, 2 * slot:2 * slot + 2, :].rearrange("p b n -> p (b n)")

        def f32(ap):
            return ap.bitcast(F32)

        def halves(b):
            return slice(HD * b, HD * b + HD), slice(HD - HD * b, P - HD * b)

        def of_pair(a, rows, hh, j):
            return a[rows, bass.ds(2 * j + hh // 2, 1), :].rearrange("p a t -> p (a t)")

        def v_of(hh, j):
            return v_plain[:, :, bass.ds(TURN_HEADS * HD * j + HD * hh, HD)]

        def y_of(g):
            rows, _ = halves(g // GROUPS_PER_HEAD % 2)
            q = g % GROUPS_PER_HEAD
            return y_f[rows, q * QG:(q + 1) * QG]

        def flat(w, part):
            return w[:, part, :, :].rearrange("p a b -> p (a b)")

        x_loaded = sem("x_loaded")
        vec_loaded = sem("vec_loaded")
        wf_loaded = sem("wf_loaded")
        wp_loaded = sem("wp_loaded")
        raw_loaded = (sem("raw_loaded_even"), sem("raw_loaded_odd"))
        attn_wo_loaded = sem("attn_wo_loaded")
        out_stored = sem("out_stored")
        consts_ready = sem("consts_ready")
        consts_cleared = sem("consts_cleared")
        wp_cleared = sem("wp_cleared")
        consts_rounded = sem("consts_rounded")
        mask_ready = sem("mask_ready")
        weights_hi = sem("weights_hi")
        weights_split = sem("weights_split")
        wp_hi = sem("wp_hi")
        wp_split = sem("wp_split")
        wf_hi = sem("wf_hi")
        wf_split = sem("wf_split")
        attn_wo_hi = sem("attn_wo_hi")
        attn_wo_split = sem("attn_wo_split")
        x_psum_ready = sem("x_psum_ready")
        x_updated = sem("x_updated")
        xg_hi = sem("xg_hi")
        xg_split = sem("xg_split")
        square_ready = sem("square_ready")
        sumsq_added = sem("sumsq_added")
        r_sum_ready = sem("r_sum_ready")
        ms_ready = sem("ms_ready")
        root_ready = sem("root_ready")
        r_col_ready = sem("r_col_ready")
        r_bcast_ready = sem("r_bcast_ready")
        r_rows_ready = sem("r_rows_ready")
        gate_ready = sem("gate_ready")
        up_ready = sem("up_ready")
        gate_scaled = sem("gate_scaled")
        sigmoid_ready = sem("sigmoid_ready")
        gated = sem("gated")
        up_scaled = sem("up_scaled")
        hidden_ready = sem("hidden_ready")
        hidden_hi = sem("hidden_hi")
        hidden_split = sem("hidden_split")
        proj_ready = sem("proj_ready")
        proj_taken = sem("proj_taken")
        pooled_ready = sem("pooled_ready")
        pooled_hi = sem("pooled_hi")
        pooled_split = sem("pooled_split")
        pool_y_hi = sem("pool_y_hi")
        conv_y_ready = sem("conv_y_ready")
        conv_y_hi = sem("conv_y_hi")
        conv_y_split = sem("conv_y_split")
        chain = sem("vector_chain")
        forget_low = sem("forget_low")
        forget_abs = sem("forget_abs")
        forget_exp = sem("forget_exp")
        forget_sum = sem("forget_sum")
        forget_log = sem("forget_log")
        forget_lost = sem("forget_lost")
        forget_inv = sem("forget_inv")
        decay_summed = sem("decay_summed")
        decay_filled = sem("decay_filled")
        decay_hi = sem("decay_hi")
        decay_lo = sem("decay_lo")
        decay_ready = sem("decay_ready")
        stack_hi = sem("stack_hi")
        stack_split = sem("stack_split")
        head_picked = sem("head_picked")
        stack_ready = sem("stack_ready")
        scores_ready = sem("scores_ready")
        max_found = sem("max_found")
        max_ready = sem("max_ready")
        exp_done = sem("exp_done")
        recip_ready = sem("recip_ready")
        prob_ready = sem("prob_ready")
        transposed = sem("transposed")
        pt_hi = sem("pt_hi")
        pt_split = sem("pt_split")
        pv_ready = sem("pv_ready")
        y_low = sem("y_low")
        y_summed = sem("y_summed")
        attn_y_hi = sem("attn_y_hi")
        attn_y_split = sem("attn_y_split")
        gained = sem("gained")
        out_psum_ready = sem("out_psum_ready")
        out_ready = (sem("out_ready_vector"), sem("out_ready_scalar"))

        UNITS = ("pool0", "pool1", "cc0", "cc1", "ch0", "ch1", "cb0", "cb1", "pm0", "pm1",
                 "v0a", "v0b", "v1a", "v1b", "f", "q0", "q1", "q2", "q3", "k0", "k1", "k2", "k3")
        SLOT = dict(zip(UNITS, (0, 1, 2, 3, 0, 1, 2, 3, 0, 1,
                                2, 3, 0, 1, 2, 3, 0, 1, 2, 3, 0, 1, 2)))
        NORM_SLOT = 3

        def done(name):
            return UNITS.index(name) + 1

        def counter(c, j):
            return lambda m, a: m * c + a + 2 * m * j

        def pair_at(base, n, j):
            return (base + n) % 2, 16 * ((base + n) // 2 + 1) + 48 * j

        block = ctx.enter_context(nc.Block())

        @block.sync
        def _(sp):
            def columns(w, col):
                return w.rearrange("(k p) f -> p k f", p=P)[:, :, bass.ds(col, PAIR)]

            def rows(w, chunk):
                return w.rearrange("(c p) d -> p c d", p=P)[:, bass.ds(chunk, 2), :]

            def load(base, n, j, src, chunks):
                slot, _ = pair_at(base, n, j)
                if base + n >= 2:
                    sp.wait_ge(weights_split, base + n - 1 + 6 * j)
                dst = raw[:, slot, :].rearrange("p (c f) -> p c f", c=chunks)
                sp.dma_start(dst, src).then_inc(raw_loaded[slot], 16)

            def swiglu(s, w_in, w_out):
                def gate_up(c, j):
                    group = counter(c, j)
                    load(N_FFN[s], gate_pair(c), j, columns(w_in, group(PAIR, 0)), KD)
                    load(N_FFN[s], gate_pair(c) + 1, j, columns(w_in, group(PAIR, F)), KD)

                def down(c, j):
                    load(N_FFN[s], down_pair(c), j, rows(w_out, counter(c, j)(2, 0)), 2)

                gate_up(0, 0)
                gate_up(1, 0)
                down(0, 0)
                with sp.Fori(0, TURNS - 1) as j:
                    for c in (1, 2):
                        gate_up(c + 1, j)
                        down(c, j)
                gate_up(GROUPS - 1, 0)
                down(GROUPS - 2, 0)
                down(GROUPS - 1, 0)

            for c in range(4):
                sp.dma_start(x_in[:, 2 * c:2 * c + 2, :],
                             x.rearrange("(c p) d -> p c d", p=P)[:, 2 * c:2 * c + 2, :])\
                    .then_inc(x_loaded, 16)
            swiglu(0, w1_in, w1_out)
            for n, src, chunks in (
                    (N_POOL, columns(wm_in, COL_POOL), KD), (N_CC, columns(wm_in, COL_CC), KD),
                    (N_CH, columns(wm_in, COL_CH), KD), (N_CB, columns(wm_in, COL_CB), KD),
                    (N_OUT_POOL, rows(wm_out, 4), 2),
                    (N_V0, columns(wm_in, COL_V), KD), (N_V1, columns(wm_in, COL_V + PAIR), KD),
                    (N_OUT_CONV, rows(wm_out, 6), 2),
                    (N_Q0, columns(wm_in, COL_Q), KD), (N_Q1, columns(wm_in, COL_Q + PAIR), KD),
                    (N_K0, columns(wm_in, COL_K), KD), (N_K1, columns(wm_in, COL_K + PAIR), KD)):
                load(0, n, 0, src, chunks)
            attn_raw = raw[:, ATTN_SLOT, :].rearrange("p (c f) -> p c f", c=2)
            sp.wait_ge(weights_split, N_K1 if N_K1 % 2 != ATTN_SLOT else N_K1 + 1)
            sp.dma_start(attn_raw, rows(wm_out, 0)).then_inc(attn_wo_loaded, 16)
            sp.wait_ge(attn_wo_split, 1)
            sp.dma_start(attn_raw, rows(wm_out, 2)).then_inc(attn_wo_loaded, 16)
            sp.wait_ge(attn_wo_split, 2)
            swiglu(1, w2_in, w2_out)
            for c in range(NT):
                sp.wait_ge(out_ready[c % 2], c // 2 + 1)
                sp.dma_start(out[c * P:(c + 1) * P, :], x_out[:, c, :]).then_inc(out_stored, 16)
            sp.wait_ge(out_stored, 16 * NT)

        @block.gpsimd
        def _(pool):
            pool.dma_start(vec[:, :], vectors).then_inc(vec_loaded, 16)
            pool.dma_start(wf_raw[:, :, :], wm_in.rearrange("(k p) f -> p k f", p=P)
                           [:, :, COL_F:COL_F + HEADS]).then_inc(wf_loaded, 16)
            pool.memset(ones2[:, :], 1.0)
            pool.memset(tri[:, :], 0.0)
            pool.memset(ident[:, :], 0.0).then_inc(consts_cleared, 1)
            pool.wait_ge(consts_cleared, 1)
            pool.affine_select(out=ident[:, :], in_=ident[:, :], compare_op=ALU.not_equal, fill=1.0,
                               base=0, pattern=[[-1, P]], channel_multiplier=1)
            pool.affine_select(out=tri[:, :], in_=tri[:, :], compare_op=ALU.is_ge, fill=MASKED,
                               base=0, pattern=[[-1, P]], channel_multiplier=1)\
                .then_inc(consts_ready, 1)
            pool.wait_ge(r_rows_ready, 2)
            pool.memset(wp_raw[:, :, :], 0.0).then_inc(wp_cleared, 1)
            pool.wait_ge(wp_cleared, 1)
            for g in range(len(WINDOWS)):
                h = (g % 2) * HD
                pool.dma_start(wp_raw[h:h + HD, g // 2, h:h + HD], w_pool[g, :, :])\
                    .then_inc(wp_loaded, 16)

        @block.scalar
        def _(act):
            def copy(dst, src, scale=1.0):
                return act.activation(dst, src, ACT.Copy, scale=scale)

            def split_hi(w, base, n, j=0):
                slot, loaded = pair_at(base, n, j)
                act.wait_ge(raw_loaded[slot], loaded)
                copy(flat(w, HI), raw[:, slot, :]).then_inc(weights_hi, 1)

            def gain_hi(before, v):
                for k in range(KD):
                    act.wait_ge(x_updated, before + k + 1)
                    act.activation(xg[:, HI, k, :], xt[:, k, :], ACT.Identity,
                                   scale=vec[:, v + k:v + k + 1]).then_inc(xg_hi, 1)

            def square(s, k):
                if k >= 2:
                    act.wait_ge(sumsq_added, (KD - 1) * s + k - 1)
                act.activation(tmp[:, min(k, 1), :], xt[:, k, :], ACT.Square)\
                    .then_inc(square_ready, 1)

            def root_step(s):
                act.wait_ge(ms_ready, s + 1)
                act.activation(root[:, :], ms[:, :], ACT.Sqrt).then_inc(root_ready, 1)

            def swiglu(s):
                base, g0, x0 = N_FFN[s], 2 * GROUPS * s, X_BASE[s]

                def hidden(c, j):
                    i = counter(c, j)
                    for f in range(2):
                        act.wait_ge(gate_scaled, i(2, g0 + f + 1))
                        act.activation(tmp[:, 1, :], tmp[:, 0, :], ACT.Sigmoid)\
                            .then_inc(sigmoid_ready, 1)
                        if f == 0 and c > 0:
                            act.wait_ge(x_psum_ready, i(KD, x0 - KD))
                        act.wait_ge(hidden_ready, i(2, g0 + f + 1))
                        copy(hid[c % 2][:, HI, f, :], tmp[:, 0, :]).then_inc(hidden_hi, 1)

                def split_gate_up(c, j):
                    i = counter(c, j)
                    act.wait_ge(gate_ready, i(2, g0))
                    split_hi(w_a, base, gate_pair(c), j)
                    act.wait_ge(up_ready, i(2, g0))
                    split_hi(w_b, base, gate_pair(c) + 1, j)

                def split_down(c, j):
                    act.wait_ge(x_psum_ready, counter(c, j)(KD, x0))
                    split_hi(w_o, base, down_pair(c), j)

                hidden(0, 0)
                split_gate_up(1, 0)
                split_down(0, 0)
                with act.Fori(0, TURNS - 1) as j:
                    for c in (1, 2):
                        hidden(c, j)
                        split_gate_up(c + 1, j)
                        split_down(c, j)
                hidden(GROUPS - 2, 0)
                split_gate_up(GROUPS - 1, 0)
                split_down(GROUPS - 2, 0)
                hidden(GROUPS - 1, 0)
                split_down(GROUPS - 1, 0)

            act.wait_ge(consts_ready, 1)
            copy(ident_r[:, :], ident[:, :])
            copy(causal_r[:, :], tri[:, :]).then_inc(consts_rounded, 1)
            act.wait_ge(vec_loaded, 16)
            gain_hi(0, V_NORM1)
            split_hi(w_a, 0, 0)
            split_hi(w_b, 0, 1)
            for k in range(KD):
                square(0, k)
            root_step(0)
            swiglu(0)

            act.wait_ge(gate_ready, 2 * GROUPS)
            split_hi(w_a, 0, N_POOL)
            act.wait_ge(up_ready, 2 * GROUPS)
            split_hi(w_b, 0, N_CC)
            gain_hi(X_MIX - KD, V_MIX)
            for k in range(KD):
                square(1, k)
            root_step(1)
            act.wait_ge(proj_ready, done("pool1"))
            split_hi(w_a, 0, N_CH)
            act.wait_ge(wp_loaded, 16 * len(WINDOWS))
            copy(wp_r[:, HI, :, :], wp_raw[:, :, :]).then_inc(wp_hi, 1)
            for c in range(2):
                act.wait_ge(pooled_ready, c + 1)
                copy(hid0[:, HI, c, :], pool_u).then_inc(pooled_hi, 1)
            act.wait_ge(proj_ready, done("cc1"))
            split_hi(w_b, 0, N_CB)
            act.wait_ge(x_psum_ready, X_MIX)
            split_hi(w_o, 0, N_OUT_POOL)
            act.wait_ge(proj_ready, done("ch1"))
            split_hi(w_a, 0, N_V0)
            act.wait_ge(proj_ready, done("cb1"))
            split_hi(w_b, 0, N_V1)
            for c in range(2):
                act.wait_ge(proj_ready, done("pm%d" % c))
                act.activation(hid0[:, HI, c, :], unit(SLOT["pm%d" % c]), ACT.Identity,
                               scale=vec[:, V_PSCALE + c:V_PSCALE + c + 1]).then_inc(pool_y_hi, 1)
            act.wait_ge(x_psum_ready, X_MIX + KD)
            act.wait_ge(conv_y_ready, 2)
            for c in range(2):
                copy(hid0[:, HI, c, :], conv_cc[:, c, :]).then_inc(conv_y_hi, 1)
            split_hi(w_o, 0, N_OUT_CONV)
            act.wait_ge(proj_ready, done("v0b"))
            act.wait_ge(wf_loaded, 16)
            copy(wf[:, :, 0:HEADS], wf_raw[:, :, :]).then_inc(wf_hi, 1)
            act.wait_ge(proj_ready, done("v1b"))
            split_hi(w_b, 0, N_Q0)
            act.wait_ge(proj_ready, done("f"))
            copy(row(0, 0), unit(SLOT["f"])[32:32 + HEADS, :]).then_inc(forget_low, 1)
            split_hi(w_a, 0, N_Q1)
            act.wait_ge(forget_abs, 1)
            act.activation(row(0, 1), row(0, 0), ACT.Exp, scale=-1.0).then_inc(forget_exp, 1)
            act.wait_ge(forget_sum, 1)
            act.activation(row(0, 2), row(1, 1), ACT.Ln).then_inc(forget_log, 1)
            act.wait_ge(forget_log, 1)
            act.wait_ge(forget_lost, 1)
            act.activation(row(0, 1), row(0, 2), ACT.Exp, scale=-1.0).then_inc(forget_inv, 1)
            act.wait_ge(proj_ready, done("q1"))
            split_hi(w_b, 0, N_K0)
            act.wait_ge(proj_ready, done("q3"))
            split_hi(w_a, 0, N_K1)

            act.wait_ge(decay_filled, 1)
            act.wait_ge(decay_summed, 1)
            copy(decay_k[0:HEADS, :], row(1, 0), 1 / SCALE).then_inc(decay_hi, 1)
            act.wait_ge(decay_hi, 1)
            copy(decay_q[64:64 + HEADS, :], f32(decay_k[0:HEADS, :]), -1.0)
            act.wait_ge(decay_lo, 1)
            copy(decay_q[96:96 + HEADS, :], f32(decay_k[32:32 + HEADS, :]), -1.0)\
                .then_inc(decay_ready, 1)
            act.wait_ge(proj_taken, done("k3"))

            def stack(hh, j):
                b = hh % 2
                own, other = halves(b)
                q, k = of_pair(q_plain, own, hh, j), of_pair(k_plain, own, hh, j)
                copy(q_st[own, b, :], q)
                copy(k_hi[other, b, :], k)
                copy(k_hi[own, b, :], k)
                copy(v_st[:, b, :, 0:HD], v_of(hh, j)).then_inc(stack_hi, 1)

            with act.Fori(0, 2) as j:
                stack(0, j)
                stack(1, j)
                act.wait_ge(attn_wo_loaded, 16 * j + 16)
                act.wait_ge(x_psum_ready, X_ATTN + 2 * KD * j)
                copy(flat(a_wo, HI), raw[:, ATTN_SLOT, :]).then_inc(attn_wo_hi, 1)
                for t in range(STEPS + 4):
                    if t < STEPS:
                        s, n = t % 2, P * (t % NT + 1)
                        if t >= 2:
                            act.wait_ge(transposed, STEPS * j + t - 1)
                        act.wait_ge(max_ready, STEPS * j + t + 1)
                        act.activation(prob[:, s, 0:n], unit(s)[:, 0:n], ACT.Exp,
                                       bias=stat[:, 1, s:s + 1], scale=SCALE,
                                       accum_out=stat[:, 2, s:s + 1]).then_inc(exp_done, 1)
                    if 1 <= t <= STEPS:
                        r = t - 1
                        nk, to = r % NT + 1, P * (r % 2)
                        act.wait_ge(transposed, STEPS * j + r + 1)
                        if r % 2 == 0 and r >= 2:
                            act.wait_ge(pv_ready, TURN_GROUPS * j + r // 2)
                        copy(pt[:, HI, 0:nk, to:to + P],
                             unit(2)[:, 0:nk * P].rearrange("p (k q) -> p k q", k=nk))\
                            .then_inc(pt_hi, 1)
                    if t >= 4 and t % 2 == 0 and t // 2 - 2 < TURN_GROUPS:
                        g = t // 2 - 2
                        act.wait_ge(pv_ready, TURN_GROUPS * j + g + 1)
                        if g == TURN_GROUPS // 2:
                            act.wait_ge(attn_y_split, 2 * j + 1)
                        copy(y_of(g), ps[HD:2 * HD, 6 + g % 2, 0:QG]).then_inc(y_low, 1)
                    if t in (2 * TURN_GROUPS // 2 + 3, 2 * TURN_GROUPS + 3):
                        pair = t // (2 * TURN_GROUPS)
                        act.wait_ge(y_summed, TURN_GROUPS * j + TURN_GROUPS // 2 * (pair + 1))
                        copy(a_y[:, HI, pair, :], y_f[:, :]).then_inc(attn_y_hi, 1)
                    if t % NT == 3 and 1 <= t // NT < TURN_HEADS - 1:
                        act.wait_ge(pv_ready, TURN_GROUPS * j + GROUPS_PER_HEAD * (t // NT))
                        stack(t // NT + 1, j)

            gain_hi(X_FFN2 - KD, V_NORM2)
            act.wait_ge(x_psum_ready, X_FFN2)
            split_hi(w_a, N_FFN[1], 0)
            split_hi(w_b, N_FFN[1], 1)
            for k in range(KD):
                square(2, k)
            root_step(2)
            swiglu(1)
            act.wait_ge(up_ready, 4 * GROUPS)
            for k in range(KD):
                act.wait_ge(x_updated, X_END - KD + k + 1)
                square(3, k)
                act.activation(x_gain[:, k, :], xt[:, k, :], ACT.Identity,
                               scale=vec[:, V_FINAL + k:V_FINAL + k + 1]).then_inc(gained, 1)
            root_step(3)
            act.wait_ge(r_col_ready, 4)
            for c in range(1, NT, 2):
                act.wait_ge(out_psum_ready, c + 1)
                act.activation(x_out[:, c, :], unit(c % 4), ACT.Identity,
                               scale=r_col[:, c:c + 1]).then_inc(out_ready[1], 1)

        @block.vector
        def _(dve):
            steps = [0]

            def link(ins):
                steps[0] += 1
                ins.then_inc(chain, 1)
                dve.wait_ge(chain, steps[0])

            def mul(dst, a, b):
                return dve.tensor_tensor(out=dst, in0=a, in1=b, op=ALU.mult)

            def add(dst, a, b):
                return dve.tensor_tensor(out=dst, in0=a, in1=b, op=ALU.add)

            def lo_part(dst, value, hi):
                return dve.tensor_tensor(out=dst, in0=value, in1=f32(hi), op=ALU.subtract)

            def scaled_lo(dst, value, scale, hi):
                return dve.scalar_tensor_tensor(out=dst, in0=value, scalar=scale, in1=f32(hi),
                                                op0=ALU.mult, op1=ALU.subtract)

            def split_lo(w, base, n, j=0):
                slot, _ = pair_at(base, n, j)
                dve.wait_ge(weights_hi, base + n + 1 + 6 * j)
                lo_part(flat(w, LO), raw[:, slot, :], flat(w, HI)).then_inc(weights_split, 1)

            def gain_lo(s, k, v):
                dve.wait_ge(xg_hi, KD * s + k + 1)
                scaled_lo(xg[:, LO, k, :], xt[:, k, :], vec[:, v + k:v + k + 1], xg[:, HI, k, :])\
                    .then_inc(xg_split, 1)

            def residual(k, factor, at_count, last_count, cols=slice(0, T), psum=None):
                dve.wait_ge(x_psum_ready, at_count)
                dve.wait_ge(x_updated, last_count)
                dve.scalar_tensor_tensor(out=xt[:, k, cols], in0=psum, scalar=factor,
                                         in1=xt[:, k, cols], op0=ALU.mult, op1=ALU.add)\
                    .then_inc(x_updated, 1)

            def sum_square(s, k):
                dve.wait_ge(square_ready, KD * s + k + 1)
                if k >= 2:
                    dve.wait_ge(sumsq_added, (KD - 1) * s + k - 1)
                add(tmp[:, 0, :], tmp[:, 0, :], tmp[:, 1, :]).then_inc(sumsq_added, 1)

            def inverse_rms(s):
                dve.wait_ge(r_sum_ready, s + 1)
                sums = ps[:, 2 * NORM_SLOT, 0:2 * NT].rearrange("p (c two) -> p c two", two=2)
                dve.tensor_scalar(ms[:, :], sums[:, :, 0], 1.0 / D, EPS, ALU.mult, ALU.add)\
                    .then_inc(ms_ready, 1)
                dve.wait_ge(root_ready, s + 1)
                link(dve.reciprocal(root[:, :], root[:, :]))
                link(mul(newton[:, :], root[:, :], root[:, :]))
                link(mul(newton[:, :], newton[:, :], ms[:, :]))
                link(dve.tensor_scalar(newton[:, :], newton[:, :], -0.5, 1.5, ALU.mult, ALU.add))
                mul(r_col[:, :], root[:, :], newton[:, :]).then_inc(r_col_ready, 1)

            def spread_rms(s):
                dve.wait_ge(r_bcast_ready, s + 1)
                dve.tensor_copy(r_rows[:, :], unit(NORM_SLOT)).then_inc(r_rows_ready, 1)
                dve.wait_ge(r_rows_ready, s + 1)

            def norm(s):
                for k in range(1, KD):
                    sum_square(s, k)
                inverse_rms(s)
                spread_rms(s)

            def swiglu(s, tail):
                base, g0, x0 = N_FFN[s], 2 * GROUPS * s, X_BASE[s]

                def hidden(c, j):
                    i = counter(c, j)
                    for f in range(2):
                        now = i(2, g0 + f + 1)
                        dve.wait_ge(gate_ready, now)
                        if c > 0 or f > 0:
                            dve.wait_ge(hidden_split, now - 1)
                        mul(tmp[:, 0, :], unit(2 * f), r_rows[:, :]).then_inc(gate_scaled, 1)
                        dve.wait_ge(sigmoid_ready, now)
                        mul(tmp[:, 0, :], tmp[:, 0, :], tmp[:, 1, :]).then_inc(gated, 1)
                        dve.wait_ge(gated, now)
                        dve.wait_ge(up_ready, now)
                        mul(tmp[:, 1, :], unit(2 * f + 1), r_rows[:, :]).then_inc(up_scaled, 1)
                        dve.wait_ge(up_scaled, now)
                        mul(tmp[:, 0, :], tmp[:, 0, :], tmp[:, 1, :]).then_inc(hidden_ready, 1)
                        dve.wait_ge(hidden_hi, now)
                        lo_part(hid[c % 2][:, LO, f, :], tmp[:, 0, :], hid[c % 2][:, HI, f, :])\
                            .then_inc(hidden_split, 1)

                def update(c, j, k):
                    i = counter(c, j)
                    residual(k, 0.5, i(KD, x0 + k + 1), i(KD, x0 + k + 1 - KD), psum=unit(k % 4))

                def split_gate(c, j):
                    split_lo(w_a, base, gate_pair(c), j)

                def split_up(c, j):
                    split_lo(w_b, base, gate_pair(c) + 1, j)

                def split_down(c, j):
                    split_lo(w_o, base, down_pair(c), j)

                def step(c, j, more):
                    hidden(c, j)
                    for k in range(KD):
                        update(c - 1, j, k)
                        if more and k == 1:
                            split_gate(c + 1, j)
                        if more and k == 3:
                            split_up(c + 1, j)
                    split_down(c, j)

                hidden(0, 0)
                split_gate(1, 0)
                split_up(1, 0)
                split_down(0, 0)
                with dve.Fori(0, TURNS - 1) as j:
                    step(1, j, True)
                    step(2, j, True)
                step(GROUPS - 2, 0, True)
                step(GROUPS - 1, 0, False)
                tail(lambda k: update(GROUPS - 1, 0, k))

            dve.wait_ge(consts_ready, 1)
            dve.tensor_reduce(head_mask[:, :], ident[:, :].rearrange("p (q h) -> p h q", q=4)
                              [:, 0:HEADS, :], AX.X, ALU.add).then_inc(mask_ready, 1)
            dve.wait_ge(vec_loaded, 16)
            for k in range(KD + 1):
                if k < KD:
                    dve.wait_ge(x_psum_ready, k + 1)
                    dve.tensor_copy(xt[:, k, :], unit(k % 4)).then_inc(x_updated, 1)
                if k > 0:
                    dve.wait_ge(x_updated, k)
                    gain_lo(0, k - 1, V_NORM1)
            split_lo(w_a, 0, 0)
            split_lo(w_b, 0, 1)
            norm(0)

            def before_mixer(update):
                split_lo(w_a, 0, N_POOL)
                split_lo(w_b, 0, N_CC)
                for k in range(KD + 1):
                    if k < KD:
                        update(k)
                    if k > 0:
                        gain_lo(1, k - 1, V_MIX)
                norm(1)

            swiglu(0, before_mixer)

            def take(name, dst):
                dve.wait_ge(proj_ready, done(name))
                return mul(dst, unit(SLOT[name]), r_rows[:, :])

            def taken_and_linked(name, ins):
                ins.then_inc(proj_taken, 1)
                dve.wait_ge(proj_taken, done(name))

            def window(dst, src, shift, rows=slice(0, P)):
                link(add(dst[rows, WMAX:], src[rows, WMAX:], src[rows, WMAX - shift:T + WMAX - shift]))

            upper = slice(HD, P)
            dve.memset(pool_a[:, 0:WMAX], 0.0)
            link(dve.memset(pool_b[:, 0:WMAX], 0.0))
            for c in range(2):
                if c > 0:
                    dve.wait_ge(pooled_split, c)
                taken_and_linked("pool%d" % c, take("pool%d" % c, pool_u))
                add(pool_a[:, WMAX + 1:], pool_u[:, 1:], pool_u[:, 0:T - 1])
                link(dve.tensor_copy(pool_a[:, WMAX:WMAX + 1], pool_u[:, 0:1]))
                if c == 0:
                    window(pool_b, pool_a, 2, upper)
                else:
                    window(pool_b, pool_a, 2)
                    window(pool_a, pool_b, 4)
                    window(pool_b, pool_a, 8, upper)
                counts = vec[:, V_COUNT + c * WMAX:V_COUNT + (c + 1) * WMAX]
                for rows, sums in ((slice(0, HD), pool_a), (upper, pool_b)):
                    dve.scalar_tensor_tensor(
                        out=pool_u[rows, WMAX:], in0=sums[rows, 2 * WMAX:],
                        scalar=counts[rows, WMAX - 1:WMAX], in1=pool_u[rows, WMAX:],
                        op0=ALU.mult, op1=ALU.subtract)
                    link(mul(sums[rows, WMAX:2 * WMAX], sums[rows, WMAX:2 * WMAX], counts[rows, :]))
                    last = dve.tensor_tensor(out=pool_u[rows, 0:WMAX], in0=sums[rows, WMAX:2 * WMAX],
                                             in1=pool_u[rows, 0:WMAX], op=ALU.subtract)
                last.then_inc(pooled_ready, 1)
                dve.wait_ge(pooled_hi, c + 1)
                lo_part(hid0[:, LO, c, :], pool_u, hid0[:, HI, c, :]).then_inc(pooled_split, 1)
                if c == 0:
                    dve.wait_ge(wp_hi, 1)
                    lo_part(wp_r[:, LO, :, :], wp_raw[:, :, :], wp_r[:, HI, :, :])\
                        .then_inc(wp_split, 1)
            split_lo(w_a, 0, N_CH)

            dve.wait_ge(pooled_split, 2)
            link(dve.memset(conv_u[:, :, 0:TAPS - 1], 0.0))
            for c in range(2):
                name = "cc%d" % c
                taken_and_linked(name, take(name, conv_cc[:, c, :]))
            split_lo(w_b, 0, N_CB)
            split_lo(w_o, 0, N_OUT_POOL)
            for c in range(2):
                name = "ch%d" % c
                u, y = conv_u[:, c, :], conv_cc[:, c, :]
                taken_and_linked(name, take(name, u[:, TAPS - 1:]))
                link(mul(u[:, TAPS - 1:], u[:, TAPS - 1:], y))
                tap = [vec[:, V_CONV + c * TAPS + w:V_CONV + c * TAPS + w + 1] for w in range(TAPS)]
                link(dve.tensor_scalar(y, u[:, TAPS - 1:], tap[TAPS - 1], None, ALU.mult))
                for w in range(TAPS - 1):
                    link(dve.scalar_tensor_tensor(out=y, in0=u[:, w:w + T], scalar=tap[w], in1=y,
                                                  op0=ALU.mult, op1=ALU.add))
            split_lo(w_a, 0, N_V0)
            for c in range(2):
                name = "cb%d" % c
                if c > 0:
                    dve.wait_ge(conv_y_ready, c)
                taken_and_linked(name, take(name, conv_b))
                mul(conv_cc[:, c, :], conv_cc[:, c, :], conv_b).then_inc(conv_y_ready, 1)
            split_lo(w_b, 0, N_V1)

            for c in range(2):
                name = "pm%d" % c
                dve.wait_ge(pool_y_hi, c + 1)
                scaled_lo(hid0[:, LO, c, :], unit(SLOT[name]),
                          vec[:, V_PSCALE + c:V_PSCALE + c + 1], hid0[:, HI, c, :])\
                    .then_inc(proj_taken, 1)
            for k in range(KD):
                now = X_MIX + k + 1
                residual(k, 1.0, now, now - KD, psum=unit((2 + k) % 4))
            for c in range(2):
                dve.wait_ge(conv_y_hi, c + 1)
                lo_part(hid0[:, LO, c, :], conv_cc[:, c, :], hid0[:, HI, c, :])\
                    .then_inc(conv_y_split, 1)
            split_lo(w_o, 0, N_OUT_CONV)
            dve.wait_ge(conv_y_split, 2)

            for n, name in enumerate(("v0a", "v0b", "v1a", "v1b")):
                dve.wait_ge(proj_ready, done(name))
                for i in range(4):
                    c = 4 * (n % 2) + i
                    last = dve.tensor_scalar(
                        v_plain[:, c, PAIR * (n // 2):PAIR * (n // 2 + 1)],
                        unit(SLOT[name])[:, i * PAIR:(i + 1) * PAIR], r_col[:, c:c + 1], None,
                        ALU.mult)
                last.then_inc(proj_taken, 1)
                if n == 1:
                    dve.wait_ge(wf_hi, 1)
                    lo_part(wf[:, :, 32:32 + HEADS], wf_raw[:, :, :], wf[:, :, 0:HEADS])\
                        .then_inc(wf_split, 1)
            split_lo(w_b, 0, N_Q0)

            dve.wait_ge(forget_low, 1)
            add(row(1, 0), unit(SLOT["f"])[0:HEADS, :], row(0, 0)).then_inc(proj_taken, 1)
            dve.wait_ge(proj_taken, done("f"))
            link(mul(row(1, 0), row(1, 0), r_rows[0:HEADS, :]))
            link(dve.tensor_scalar(row(1, 0), row(1, 0), vec[0:HEADS, V_BFORGET:V_BFORGET + 1],
                                   None, ALU.add))
            dve.scalar_tensor_tensor(out=row(0, 0), in0=row(1, 0), scalar=-1.0, in1=row(1, 0),
                                     op0=ALU.mult, op1=ALU.max).then_inc(forget_abs, 1)
            split_lo(w_a, 0, N_Q1)
            dve.wait_ge(forget_exp, 1)
            dve.tensor_scalar(row(1, 1), row(0, 1), 1.0, None, ALU.add).then_inc(forget_sum, 1)
            dve.wait_ge(forget_log, 1)
            dve.scalar_tensor_tensor(out=row(1, 1), in0=row(1, 1), scalar=-1.0, in1=row(0, 1),
                                     op0=ALU.add, op1=ALU.subtract).then_inc(forget_lost, 1)
            dve.wait_ge(forget_inv, 1)
            link(mul(row(1, 2), row(1, 1), row(0, 1)))
            link(dve.tensor_tensor(out=row(0, 2), in0=row(0, 2), in1=row(1, 2), op=ALU.subtract))
            link(dve.tensor_scalar(row(1, 2), row(1, 0), -1.0, 0.0, ALU.mult, ALU.max))
            dve.tensor_tensor_scan(row(1, 0), row(1, 2), row(0, 2), 0.0, ALU.add, ALU.add)\
                .then_inc(decay_summed, 1)

            for k in range(KD):
                now = X_MIX + KD + k + 1
                residual(k, 1.0, now, now - KD, psum=unit((3 + k) % 4))
            for n, (part, pair) in enumerate(((q_plain, 0), (q_plain, 2), (k_plain, 0), (k_plain, 2))):
                for i in range(2):
                    name = ("q%d" if part is q_plain else "k%d") % (pair + i)
                    take(name, part[:, pair + i, :]).then_inc(proj_taken, 1)
                if n == 0:
                    split_lo(w_b, 0, N_K0)
                if n == 1:
                    split_lo(w_a, 0, N_K1)

            dve.memset(f32(decay_k[:, :]), 1.0)
            dve.memset(f32(decay_q[:, :]), 1.0).then_inc(decay_filled, 1)
            dve.wait_ge(decay_summed, 1)
            dve.wait_ge(decay_hi, 1)
            scaled_lo(decay_k[32:32 + HEADS, :], row(1, 0), 1 / SCALE, decay_k[0:HEADS, :])\
                .then_inc(decay_lo, 1)
            dve.wait_ge(mask_ready, 1)
            dve.wait_ge(decay_ready, 1)
            dve.wait_ge(proj_taken, done("k3"))

            def stack(hh, j):
                b = hh % 2
                own, other = halves(b)
                q, k = of_pair(q_plain, own, hh, j), of_pair(k_plain, own, hh, j)
                dve.wait_ge(stack_hi, TURN_HEADS * j + hh + 1)
                lo_part(q_st[other, b, :], q, q_st[own, b, :])
                lo_part(k_lo[own, b, :], k, k_hi[own, b, :])
                lo_part(k_lo[other, b, :], k, k_hi[own, b, :])
                lo_part(v_st[:, b, :, HD:2 * HD], v_of(hh, j), v_st[:, b, :, 0:HD])\
                    .then_inc(stack_split, 1)

            def decay(hh, j):
                if hh > 0:
                    dve.wait_ge(stack_ready, TURN_HEADS * j + hh)
                dve.tensor_copy(head_col[:, :], head_mask[:, bass.ds(TURN_HEADS * j + hh, 1)])\
                    .then_inc(head_picked, 1)
                dve.wait_ge(head_picked, TURN_HEADS * j + hh + 1)
                dve.tensor_scalar(decay_h[:, :], f32(decay_k[:, :]), head_col[:, 0:1], None,
                                  ALU.mult).then_inc(stack_ready, 1)

            with dve.Fori(0, 2) as j:
                stack(0, j)
                decay(0, j)
                stack(1, j)
                dve.wait_ge(attn_wo_hi, j + 1)
                lo_part(flat(a_wo, LO), raw[:, ATTN_SLOT, :], flat(a_wo, HI))\
                    .then_inc(attn_wo_split, 1)
                for t in range(STEPS + 4):
                    if t < STEPS:
                        s, n = t % 2, P * (t % NT + 1)
                        dve.wait_ge(scores_ready, STEPS * j + t + 1)
                        dve.tensor_reduce(stat[:, 0, s:s + 1], unit(s)[:, 0:n], AX.X, ALU.max)\
                            .then_inc(max_found, 1)
                        dve.wait_ge(max_found, STEPS * j + t + 1)
                        dve.tensor_scalar(stat[:, 1, s:s + 1], stat[:, 0, s:s + 1], -SCALE, None,
                                          ALU.mult).then_inc(max_ready, 1)
                        if t % NT == NT - 1 and t < STEPS - 1:
                            decay(t // NT + 1, j)
                    if 1 <= t <= STEPS:
                        r = t - 1
                        s, n = r % 2, P * (r % NT + 1)
                        dve.wait_ge(exp_done, STEPS * j + r + 1)
                        dve.reciprocal(stat[:, 3, s:s + 1], stat[:, 2, s:s + 1])\
                            .then_inc(recip_ready, 1)
                        dve.wait_ge(recip_ready, STEPS * j + r + 1)
                        dve.tensor_scalar(prob[:, s, 0:n], prob[:, s, 0:n], stat[:, 3, s:s + 1],
                                          None, ALU.mult).then_inc(prob_ready, 1)
                    if 2 <= t <= STEPS + 1:
                        r = t - 2
                        nk, to = r % NT + 1, P * (r % 2)
                        dve.wait_ge(pt_hi, STEPS * j + r + 1)
                        lo_part(pt[:, LO, 0:nk, to:to + P],
                                unit(2)[:, 0:nk * P].rearrange("p (k q) -> p k q", k=nk),
                                pt[:, HI, 0:nk, to:to + P]).then_inc(pt_split, 1)
                    if t >= 4 and t % 2 == 0 and t // 2 - 2 < TURN_GROUPS:
                        g = t // 2 - 2
                        dve.wait_ge(y_low, TURN_GROUPS * j + g + 1)
                        add(y_of(g), ps[0:HD, 6 + g % 2, 0:QG], y_of(g)).then_inc(y_summed, 1)
                    if t in (2 * TURN_GROUPS // 2 + 3, 2 * TURN_GROUPS + 3):
                        pair = t // (2 * TURN_GROUPS)
                        dve.wait_ge(attn_y_hi, 2 * j + pair + 1)
                        lo_part(a_y[:, LO, pair, :], y_f[:, :], a_y[:, HI, pair, :])\
                            .then_inc(attn_y_split, 1)
                    if t % NT == 4 and 1 <= t // NT < TURN_HEADS - 1:
                        stack(t // NT + 1, j)
                for n in range(2 * KD):
                    half = slice(BANK * (n % 2), BANK * (n % 2 + 1))
                    now = X_ATTN + n + 1 + 2 * KD * j
                    residual(n // 2, 1.0, now, now - KD, half, ps[:, 6 + n % 2, :])

            for k in range(KD):
                gain_lo(2, k, V_NORM2)
            split_lo(w_a, N_FFN[1], 0)
            split_lo(w_b, N_FFN[1], 1)
            norm(2)

            def before_output(update):
                for k in range(KD + 1):
                    if k < KD:
                        update(k)
                    if k > 1:
                        sum_square(3, k - 1)
                inverse_rms(3)

            swiglu(1, before_output)
            dve.wait_ge(r_col_ready, 4)
            for c in range(0, NT, 2):
                dve.wait_ge(out_psum_ready, c + 1)
                dve.tensor_scalar(x_out[:, c, :], unit(c % 4), r_col[:, c:c + 1], None, ALU.mult)\
                    .then_inc(out_ready[0], 1)

        @block.tensor
        def _(pe):
            def projection(slot, w, chunk, ready):
                for half in range(2):
                    for k in range(KD):
                        for a, b in PASSES:
                            last = pe.matmul(ps[:, 2 * slot + half, :],
                                             w[:, a, k, chunk * P:(chunk + 1) * P],
                                             xg[:, b, k, half * BANK:(half + 1) * BANK],
                                             start=(k == 0 and (a, b) == PASSES[0]),
                                             stop=(k == KD - 1 and (a, b) == PASSES[-1]))
                last.then_inc(ready, 1)

            def output(bank, w, y, k, half):
                for f in range(2):
                    for a, b in PASSES:
                        last = pe.matmul(ps[:, bank, :], w[:, a, f, k * P:(k + 1) * P],
                                         y[:, b, f, half * BANK:(half + 1) * BANK],
                                         start=(f == 0 and (a, b) == PASSES[0]),
                                         stop=(f == 1 and (a, b) == PASSES[-1]))
                return last

            def sum_rows(s):
                pe.wait_ge(sumsq_added, (KD - 1) * (s + 1))
                for c in range(NT):
                    last = pe.matmul(ps[:, 2 * NORM_SLOT, 2 * c:2 * c + 2],
                                     tmp[:, 0, c * P:(c + 1) * P], ones2[:, :],
                                     start=True, stop=True)
                last.then_inc(r_sum_ready, 1)

            def spread_rows(s):
                pe.wait_ge(r_col_ready, s + 1)
                for c in range(NT):
                    last = pe.matmul(ps[:, 2 * NORM_SLOT + c // 4, c % 4 * P:(c % 4 + 1) * P],
                                     r_col[:, c:c + 1].to_broadcast([P, P]), ident[:, :],
                                     start=True, stop=True)
                last.then_inc(r_bcast_ready, 1)

            def swiglu(s):
                base, g0, x0 = N_FFN[s], 2 * GROUPS * s, X_BASE[s]

                def hidden(c, j):
                    i = counter(c, j)
                    for f in range(2):
                        if f == 0:
                            pe.wait_ge(weights_split, base + gate_pair(c) + 1 + 6 * j)
                        if c > 0:
                            pe.wait_ge(x_updated, i(KD, x0 - 2 * KD + 5 + 2 * f))
                            pe.wait_ge(gate_scaled, i(2, g0 + f - 1))
                        projection(2 * f, w_a, f, gate_ready)
                        if c == 0 and f == 1:
                            spread_rows(2 * s)
                            pe.wait_ge(r_rows_ready, 2 * s + 1)
                        if f == 0:
                            pe.wait_ge(weights_split, base + gate_pair(c) + 2 + 6 * j)
                        if c > 0:
                            pe.wait_ge(x_updated, i(KD, x0 - 2 * KD + 6 + 2 * f))
                            pe.wait_ge(up_scaled, i(2, g0 + f - 1))
                        projection(2 * f + 1, w_b, f, up_ready)
                        if c == 0 and f == 0:
                            sum_rows(2 * s)

                def down(c, j, last_group=False):
                    i = counter(c, j)
                    pe.wait_ge(weights_split, base + down_pair(c) + 1 + 6 * j)
                    pe.wait_ge(hidden_split, i(2, g0 + 2))
                    for k in range(KD):
                        if k >= 4 or last_group:
                            pe.wait_ge(x_updated, i(KD, x0 + k - 3))
                        else:
                            pe.wait_ge((gate_scaled, up_scaled)[k % 2], i(2, g0 + 3 + k // 2))
                        for half in range(2):
                            last = output(2 * (k % 4) + half, w_o, hid[c % 2], k, half)
                        last.then_inc(x_psum_ready, 1)

                pe.wait_ge(xg_split, KD * (2 * s + 1))
                hidden(0, 0)
                with pe.Fori(0, TURNS) as j:
                    hidden(1, j)
                    down(0, j)
                    hidden(2, j)
                    down(1, j)
                down(GROUPS - 1, 0, True)

            pe.wait_ge(consts_ready, 1)
            pe.wait_ge(x_loaded, 64)
            for k in range(KD):
                if k >= 4:
                    pe.wait_ge(x_updated, k - 3)
                for c in range(NT):
                    last = pe.transpose(unit(k % 4)[:, c * P:(c + 1) * P],
                                        x_in[:, c, k * P:(k + 1) * P], ident[:, :])
                last.then_inc(x_psum_ready, 1)
            swiglu(0)

            pe.wait_ge(xg_split, 2 * KD)
            pe.wait_ge(weights_split, N_POOL + 1)
            projection(0, w_a, 0, proj_ready)
            projection(1, w_a, 1, proj_ready)
            sum_rows(1)
            pe.wait_ge(weights_split, N_CC + 1)
            projection(2, w_b, 0, proj_ready)
            spread_rows(1)
            pe.wait_ge(r_rows_ready, 2)
            projection(3, w_b, 1, proj_ready)

            def pair(w, n, names, before):
                pe.wait_ge(weights_split, n + 1)
                for i, name in enumerate(names):
                    pe.wait_ge(proj_taken, done(before[i]))
                    projection(SLOT[name], w, i, proj_ready)

            pair(w_a, N_CH, ("ch0", "ch1"), ("pool0", "pool1"))
            pair(w_b, N_CB, ("cb0", "cb1"), ("cc0", "cc1"))
            pe.wait_ge(wp_split, 1)
            for c in range(2):
                pe.wait_ge(pooled_split, c + 1)
                pe.wait_ge(proj_taken, done("ch%d" % c))
                for half in range(2):
                    for a, b in PASSES:
                        last = pe.matmul(ps[:, 2 * SLOT["pm%d" % c] + half, :], wp_r[:, a, c, :],
                                         hid0[:, b, c, half * BANK:(half + 1) * BANK],
                                         start=(a, b) == PASSES[0], stop=(a, b) == PASSES[-1])
                last.then_inc(proj_ready, 1)

            def outputs(n, first_slot, x0, before):
                pe.wait_ge(weights_split, n + 1)
                for k in range(KD):
                    if k < 4:
                        pe.wait_ge(proj_taken, done(before[k]))
                    else:
                        pe.wait_ge(x_updated, x0 + k - 3)
                    for half in range(2):
                        last = output(2 * ((first_slot + k) % 4) + half, w_o, hid0, k, half)
                    last.then_inc(x_psum_ready, 1)

            pe.wait_ge(proj_taken, done("pm1"))
            outputs(N_OUT_POOL, 2, X_MIX, ("cb0", "cb1", "pm0", "pm1"))
            for n, name in enumerate(("v0a", "v0b", "v1a", "v1b")):
                w = (w_a, w_b)[n // 2]
                pe.wait_ge(weights_split, (N_V0, N_V1)[n // 2] + 1)
                pe.wait_ge(x_updated, X_MIX + KD - 3 + n)
                for i in range(4):
                    c = 4 * (n % 2) + i
                    for k in range(KD):
                        for a, b in PASSES:
                            last = pe.matmul(unit(SLOT[name])[:, i * PAIR:(i + 1) * PAIR],
                                             xg[:, b, k, c * P:(c + 1) * P], w[:, a, k, :],
                                             start=(k == 0 and (a, b) == PASSES[0]),
                                             stop=(k == KD - 1 and (a, b) == PASSES[-1]))
                last.then_inc(proj_ready, 1)
            pe.wait_ge(wf_split, 1)
            pe.wait_ge(proj_taken, done("v0a"))
            for half in range(2):
                for k in range(KD):
                    for b in (LO, HI):
                        last = pe.matmul(ps[:, 2 * SLOT["f"] + half, :], wf[:, k, :],
                                         xg[:, b, k, half * BANK:(half + 1) * BANK],
                                         start=(k == 0 and b == LO), stop=(k == KD - 1 and b == HI))
            last.then_inc(proj_ready, 1)
            pe.wait_ge(conv_y_split, 2)
            outputs(N_OUT_CONV, 3, X_MIX + KD, ("v0b", "v1a", "v1b", "f"))
            for n, (w, pairs, names) in enumerate((
                    (w_b, N_Q0, ("q0", "q1")), (w_a, N_Q1, ("q2", "q3")),
                    (w_b, N_K0, ("k0", "k1")), (w_a, N_K1, ("k2", "k3")))):
                pe.wait_ge(weights_split, pairs + 1)
                for i, name in enumerate(names):
                    if n < 2:
                        pe.wait_ge(x_updated, X_MIX + 2 * KD - 3 + 2 * n + i)
                    else:
                        pe.wait_ge(proj_taken, done("q%d" % (2 * (n - 2) + i)))
                    projection(SLOT[name], w, i, proj_ready)

            pe.wait_ge(proj_taken, done("k3"))
            pe.wait_ge(consts_rounded, 1)
            with pe.Fori(0, 2) as j:
                for t in range(STEPS + 2):
                    if t < STEPS:
                        hh, qb, s = t // NT, t % NT, t % 2
                        b, n = hh % 2, P * (qb + 1)
                        if qb == 0:
                            pe.wait_ge(stack_ready, TURN_HEADS * j + hh + 1)
                            pe.wait_ge(stack_split, TURN_HEADS * j + hh + 1)
                        if t >= 2:
                            pe.wait_ge(exp_done, STEPS * j + t - 1)
                        queries = slice(qb * P, (qb + 1) * P)
                        for bank in range((n + BANK - 1) // BANK):
                            keys = slice(bank * BANK, min(n, (bank + 1) * BANK))
                            diagonal = keys.stop == n
                            dst = unit(s)[:, keys]
                            pe.matmul(dst, q_st[:, b, queries], k_lo[:, b, keys],
                                      start=True, stop=False)
                            pe.matmul(dst, q_st[:, b, queries], k_hi[:, b, keys],
                                      start=False, stop=False)
                            last = pe.matmul(dst, decay_q[:, queries], decay_h[:, keys],
                                             start=False, stop=not diagonal)
                        last = pe.matmul(unit(s)[:, queries], ident_r[:, :], causal_r[:, :],
                                         start=False, stop=True)
                        last.then_inc(scores_ready, 1)
                    if 1 <= t <= STEPS:
                        r = t - 1
                        pe.wait_ge(prob_ready, STEPS * j + r + 1)
                        if r >= 1:
                            pe.wait_ge(pt_split, STEPS * j + r)
                        for c in range(r % NT + 1):
                            last = pe.transpose(unit(2)[:, c * P:(c + 1) * P],
                                                prob[:, r % 2, c * P:(c + 1) * P], ident[:, :])
                        last.then_inc(transposed, 1)
                    if t >= 3 and t % 2 == 1:
                        g = (t - 3) // 2
                        b, q = g // GROUPS_PER_HEAD % 2, g % GROUPS_PER_HEAD
                        pe.wait_ge(pt_split, STEPS * j + 2 * g + 2)
                        if g >= 2:
                            pe.wait_ge(y_summed, TURN_GROUPS * j + g - 1)
                        chunks = 2 * q + 2
                        for c in range(chunks):
                            start = max(0, c * P - q * QG)
                            for part in (LO, HI):
                                last = pe.matmul(ps[:, 6 + g % 2, start:QG], v_st[:, b, c, :],
                                                 pt[:, part, c, start:QG],
                                                 start=(c == 0 and part == LO),
                                                 stop=(c == chunks - 1 and part == HI))
                        last.then_inc(pv_ready, 1)
                pe.wait_ge(attn_y_split, 2 * j + 2)
                pe.wait_ge(attn_wo_split, j + 1)
                pe.wait_ge(y_summed, TURN_GROUPS * j + TURN_GROUPS)
                for n in range(2 * KD):
                    if n >= 2:
                        pe.wait_ge(x_updated, X_ATTN + n - 1 + 2 * KD * j)
                    output(6 + n % 2, a_wo, a_y, n // 2, n % 2).then_inc(x_psum_ready, 1)

            swiglu(1)

            sum_rows(3)
            for c in range(NT):
                if c == 3:
                    pe.wait_ge(r_col_ready, 4)
                if c >= 4:
                    pe.wait_ge(out_ready[c % 2], c // 2 - 1)
                pe.wait_ge(gained, KD)
                for k in range(KD):
                    last = pe.transpose(unit(c % 4)[:, k * P:(k + 1) * P],
                                        x_gain[:, k, c * P:(c + 1) * P], ident[:, :])
                last.then_inc(out_psum_ready, 1)


def kernel(**inputs):
    import numpy as np
    import concourse.bacc as bacc
    from concourse.bass_utils import run_bass_kernel_spmd

    def chunked(a):
        return np.ascontiguousarray(np.asarray(a).reshape(-1, P).T)

    inv_counts = np.zeros((P, 2, WMAX), np.float32)
    for g, w in enumerate(WINDOWS):
        rows = slice((g % 2) * HD, (g % 2 + 1) * HD)
        inv_counts[rows, g // 2, :] = 1.0 / np.minimum(np.arange(WMAX) + 1, w)
    forget = np.zeros((P, 1), np.float32)
    forget[:HEADS, 0] = np.asarray(inputs["b_forget"])[0]
    taps = np.asarray(inputs["conv_w"])[0].reshape(TAPS, 2, P).transpose(2, 1, 0)
    vectors = np.concatenate(
        [chunked(inputs[n]) for n in ("norm_ffn1", "norm_mix", "norm_ffn2", "norm_final")]
        + [taps.reshape(P, 2 * TAPS), chunked(inputs["pool_scale"]), forget,
           inv_counts.reshape(P, 2 * WMAX)], axis=1)
    arrays = {
        "x": np.asarray(inputs["x"])[0],
        "w1_in": np.asarray(inputs["w_ffn1_in"])[0], "w1_out": np.asarray(inputs["w_ffn1_out"])[0],
        "wm_in": np.asarray(inputs["w_mix_in"])[0], "wm_out": np.asarray(inputs["w_mix_out"])[0],
        "w_pool": np.asarray(inputs["w_pool"])[0],
        "w2_in": np.asarray(inputs["w_ffn2_in"])[0], "w2_out": np.asarray(inputs["w_ffn2_out"])[0],
        "vectors": vectors,
    }
    nc = bacc.Bacc("TRN2", target_bir_lowering=False, num_devices=1)
    arrays = {"in_" + n: np.ascontiguousarray(a) for n, a in arrays.items()}
    args = [nc.dram_tensor(n, a.shape, mybir.dt.from_np(a.dtype), kind="ExternalInput").ap()
            for n, a in arrays.items()]
    out = nc.dram_tensor("out_x", (T, D), F32, kind="ExternalOutput").ap()
    trunk(nc, *args, out)
    result = run_bass_kernel_spmd(nc, [arrays], core_ids=[0])
    return result.results[0]["out_x"].reshape(1, T, D)
```

```python
from contextlib import ExitStack

import concourse.bass as bass
from concourse import mybir

F32 = mybir.dt.float32
F32R = mybir.dt.float32r
ALU = mybir.AluOpType
ACT = mybir.ActivationFunctionType
AX = mybir.AxisListType

P = 128
D = 1024
T = 1024
KD = D // P
NT = T // P
BANK = 512
F = 2816
PAIR = 2 * P
GROUPS = F // PAIR
TURNS = (GROUPS - 1) // 2
HEADS = 8
HD = 64
D_ATTN = HEADS * HD
COL_Q, COL_K, COL_V = 0, D_ATTN, 2 * D_ATTN
COL_F = 3 * D_ATTN
COL_POOL = COL_F + HEADS
COL_CB = COL_POOL + PAIR
COL_CC = COL_CB + PAIR
COL_CH = COL_CC + PAIR
WINDOWS = (2, 4, 8, 16)
WMAX = WINDOWS[-1]
TAPS = 3
EPS = 1e-6
SCALE = HD ** -0.5
MASKED = -1.0e30
HI, LO = 0, 1
PASSES = ((LO, HI), (HI, LO), (HI, HI))

V_NORM1, V_MIX, V_NORM2, V_FINAL = 0, KD, 2 * KD, 3 * KD
V_CONV = 4 * KD
V_PSCALE = V_CONV + 2 * TAPS
V_BFORGET = V_PSCALE + 2
V_COUNT = V_BFORGET + 1
V_ALL = V_COUNT + 2 * WMAX

(N_POOL, N_CC, N_CH, N_CB, N_OUT_POOL, N_V0, N_V1, N_OUT_CONV,
 N_Q0, N_Q1, N_K0, N_K1, N_OUT_A0, N_OUT_A1) = range(3 * GROUPS, 3 * GROUPS + 14)
N_FFN = (0, N_OUT_A1 + 1)

X_FFN1 = KD
X_MIX = X_FFN1 + KD * GROUPS
X_ATTN = X_MIX + 2 * KD
X_FFN2 = X_ATTN + KD
X_END = X_FFN2 + KD * GROUPS
X_BASE = (X_FFN1, X_FFN2)

LAG = 3
QG = 2 * P
STEPS = HEADS * NT
TURN = 2 * NT
HEAD_GROUPS = T // QG
TURN_GROUPS = 2 * HEAD_GROUPS
FILL = 11
LOOPS = STEPS // TURN - 1
ITERATIONS = STEPS + 7
Y_HI_AT, Y_LO_AT = (1, 5), (2, 6)
PROBS = 4

KB = 1024
SBUF_START, SBUF_END = 16512, 229344


def gate_pair(g):
    return 3 * g - 1 if g else 0


def down_pair(g):
    return 3 * g + 4 if g < GROUPS - 1 else 3 * GROUPS - 1


def trunk(nc, x, w1_in, w1_out, wm_in, wm_out, w_pool, w2_in, w2_out, vectors, out):
    with ExitStack() as ctx:
        def sem(name):
            return ctx.enter_context(nc.semaphore(name))

        place = [SBUF_START]

        def at(offset, name, shape, dt):
            size = 4
            for n in shape[1:]:
                size *= n
            assert offset + size <= SBUF_END, (name, offset + size - SBUF_END)
            return nc.alloc_sbuf_tensor_at(name, shape, dt, offset=offset)

        def keep(name, shape, dt):
            size = 4
            for n in shape[1:]:
                size *= n
            offset = place[0]
            place[0] += (size + 31) // 32 * 32
            return at(offset, name, shape, dt)

        xt = keep("xt", [P, KD, T], F32)
        r_rows = keep("r_rows", [P, T], F32)
        raw = keep("raw", [P, 2, KD * PAIR], F32)
        vec = keep("vec", [P, V_ALL], F32)
        ident = keep("ident", [P, P], F32)
        ident_r = keep("ident_r", [P, P], F32R)
        causal_r = keep("causal_r", [P, P], F32R)
        tri = keep("tri", [P, P], F32)
        ones2 = keep("ones2", [P, 2], F32)
        head_mask = keep("head_mask", [P, HEADS], F32)
        ms = keep("ms", [P, NT], F32)
        root = keep("root", [P, NT], F32)
        newton = keep("newton", [P, NT], F32)
        r_col = keep("r_col", [P, NT], F32)
        sums_x = keep("sums_x", [P, NT], F32)
        row_max = keep("row_max", [P, 2], F32)
        exp_bias = keep("exp_bias", [P, 2], F32)
        exp_sum = keep("exp_sum", [P, PROBS], F32)
        exp_inv = keep("exp_inv", [P, PROBS], F32)
        head_col = keep("head_col", [P, 1], F32)
        wf_raw = keep("wf_raw", [P, KD, HEADS], F32)

        a0 = place[0]
        xg = at(a0, "xg", [P, 2, KD, T], F32R)
        w_a = at(a0 + 64 * KB, "w_a", [P, 2, KD, PAIR], F32R)
        w_b = at(a0 + 80 * KB, "w_b", [P, 2, KD, PAIR], F32R)
        w_o = at(a0 + 96 * KB, "w_o", [P, 2, 2, D], F32R)
        hid0 = at(a0 + 112 * KB, "hid0", [P, 2, 2, T], F32R)
        hid1 = at(a0 + 128 * KB, "hid1", [P, 2, 2, T], F32R)
        tmp = at(a0 + 144 * KB, "tmp", [P, 2, T], F32)
        hid = (hid0, hid1)
        x_in = at(a0 + 96 * KB, "x_in", [P, NT, D], F32)
        x_squares = at(a0 + 64 * KB, "x_squares", [P, NT, D], F32)
        mix = at(a0 + 128 * KB, "mix", [P, 5 * T + 32], F32)
        wp_raw = at(a0 + 149 * KB, "wp_raw", [P, 2, P], F32)
        wp_r = at(a0 + 150 * KB, "wp_r", [P, 2, 2, P], F32R)
        v_plain = at(a0 + 128 * KB, "v_plain", [P, NT, D_ATTN], F32)
        q_plain = at(a0 + 96 * KB, "q_plain", [P, 4, T], F32)
        k_plain = at(a0 + 112 * KB, "k_plain", [P, 4, T], F32)
        q_st = at(a0 + 0 * KB, "q_st", [P, 2, T], F32R)
        k_hi = at(a0 + 8 * KB, "k_hi", [P, 2, T], F32R)
        k_lo = at(a0 + 16 * KB, "k_lo", [P, 2, T], F32R)
        v_st = at(a0 + 24 * KB, "v_st", [P, 2, NT, 2 * HD], F32R)
        decay_k = at(a0 + 32 * KB, "decay_k", [P, T], F32R)
        decay_h = at(a0 + 36 * KB, "decay_h", [P, 2, T], F32R)
        decay_q = at(a0 + 44 * KB, "decay_q", [P, T], F32R)
        pt = at(a0 + 48 * KB, "pt", [P, 2, NT, QG], F32R)
        prob = at(a0 + 64 * KB, "prob", [P, PROBS, T], F32)
        out_w = (at(a0 + 80 * KB, "out_w0", [P, 2, 2, D], F32R),
                 at(a0 + 128 * KB, "out_w1", [P, 2, 2, D], F32R))
        y_hi = at(a0 + 96 * KB, "y_hi", [P, 4, T], F32R)
        y_lo = at(a0 + 112 * KB, "y_lo", [P, 4, T], F32R)
        y_f = tmp[:, 0, :]
        x_gain = at(a0, "x_gain", [P, KD, T], F32)
        x_out = at(a0 + 32 * KB, "x_out", [P, NT, D], F32)

        wf = w_a[:, HI, :, 0:P]

        def row(s, quadrant):
            return tmp[32 * quadrant:32 * quadrant + HEADS, s, :]

        pool_u = mix[:, 0:T]
        pool_a = mix[:, T:2 * T + WMAX]
        pool_b = mix[:, 2 * T + WMAX:3 * T + 2 * WMAX]
        conv_cc = mix[:, 3 * T + 32:5 * T + 32].rearrange("p (c t) -> p c t", c=2)
        conv_u = mix[:, 0:2 * (T + 2)].rearrange("p (c t) -> p c t", c=2)
        conv_b = mix[:, 2 * T + 16:3 * T + 16]

        ps = ctx.enter_context(nc.psum_tensor("ps", [P, 8, BANK], F32))

        def unit(slot):
            return ps[:, 2 * slot:2 * slot + 2, :].rearrange("p b n -> p (b n)")

        def f32(ap):
            return ap.bitcast(F32)

        def halves(b):
            return slice(HD * b, HD * b + HD), slice(HD - HD * b, P - HD * b)

        def of_pair(a, rows, h, j):
            return a[rows, bass.ds(h // 2 + j, 1), :].rearrange("p a t -> p (a t)")

        def v_of(h, j):
            return v_plain[:, :, bass.ds(HD * h + 2 * HD * j, HD)]

        def y_of(g):
            rows, _ = halves(g // HEAD_GROUPS % 2)
            q = g % HEAD_GROUPS
            return y_f[rows, q * QG:(q + 1) * QG]

        def pipeline(engine, iteration):
            for t in range(FILL):
                iteration(t, 0)
            with engine.Fori(0, LOOPS) as j:
                for t in range(FILL, FILL + TURN):
                    iteration(t, j)
            for t in range(FILL + LOOPS * TURN, ITERATIONS):
                iteration(t, 0)

        def blocks(t, offset):
            h, rest = divmod(t - offset, NT)
            return h + 1 if rest == 0 and 0 <= h + 1 < HEADS else None

        def banks_done(r, j, bank=1):
            count = [min(i, 4) + 2 * max(i - 4, 0) for i in range(NT + 1)]
            return (r // NT * count[NT] + (count[r % NT] + 1 if bank == 0 else count[r % NT + 1])
                    + 2 * count[NT] * j)

        def pt_banks(r):
            nk = r % NT + 1
            return [(0, slice(0, min(nk, 4)))] + ([(1, slice(4, nk))] if nk > 4 else [])

        def chunks_in_psum(keys):
            return unit(2)[:, keys.start * P:keys.stop * P]\
                .rearrange("p (k q) -> p k q", k=keys.stop - keys.start)

        def steps_done(r, j):
            return r + 1 + TURN * j

        def groups_done(g, j):
            return g + 1 + TURN_GROUPS * j

        def heads_done(h, j, parts=1):
            return parts * (h + 1) + parts * 2 * j

        def flat(w, part):
            return w[:, part, :, :].rearrange("p a b -> p (a b)")

        x_loaded = [sem("x_loaded%d" % c) for c in range(4)]
        vec_loaded = sem("vec_loaded")
        wf_loaded = sem("wf_loaded")
        wp_loaded = sem("wp_loaded")
        raw_loaded = (sem("raw_loaded_even"), sem("raw_loaded_odd"))
        out_stored = sem("out_stored")
        consts_ready = sem("consts_ready")
        consts_cleared = sem("consts_cleared")
        wp_cleared = sem("wp_cleared")
        consts_rounded = sem("consts_rounded")
        mask_ready = sem("mask_ready")
        weights_hi = sem("weights_hi")
        weights_split = sem("weights_split")
        wp_hi = sem("wp_hi")
        wp_split = sem("wp_split")
        wf_hi = sem("wf_hi")
        wf_split = sem("wf_split")
        x_psum_ready = sem("x_psum_ready")
        x_updated = sem("x_updated")
        xg_hi = sem("xg_hi")
        xg_split = sem("xg_split")
        square_ready = sem("square_ready")
        input_squared = sem("input_squared")
        sumsq_added = sem("sumsq_added")
        r_sum_ready = sem("r_sum_ready")
        ms_ready = sem("ms_ready")
        root_ready = sem("root_ready")
        r_col_ready = sem("r_col_ready")
        r_bcast_ready = sem("r_bcast_ready")
        r_rows_ready = sem("r_rows_ready")
        gate_ready = sem("gate_ready")
        up_ready = sem("up_ready")
        gate_scaled = sem("gate_scaled")
        sigmoid_ready = sem("sigmoid_ready")
        gated = sem("gated")
        up_scaled = sem("up_scaled")
        hidden_ready = sem("hidden_ready")
        hidden_hi = sem("hidden_hi")
        hidden_split = sem("hidden_split")
        proj_ready = sem("proj_ready")
        proj_taken = sem("proj_taken")
        pooled_ready = sem("pooled_ready")
        pooled_hi = sem("pooled_hi")
        pooled_split = sem("pooled_split")
        pool_y_hi = sem("pool_y_hi")
        conv_y_ready = sem("conv_y_ready")
        conv_y_hi = sem("conv_y_hi")
        conv_y_split = sem("conv_y_split")
        chain = sem("vector_chain")
        forget_low = sem("forget_low")
        forget_abs = sem("forget_abs")
        forget_exp = sem("forget_exp")
        forget_sum = sem("forget_sum")
        forget_log = sem("forget_log")
        forget_lost = sem("forget_lost")
        forget_inv = sem("forget_inv")
        decay_summed = sem("decay_summed")
        decay_filled = sem("decay_filled")
        decay_hi = sem("decay_hi")
        decay_lo = sem("decay_lo")
        decay_ready = sem("decay_ready")
        key_hi = sem("key_hi")
        query_hi = sem("query_hi")
        value_hi = sem("value_hi")
        key_lo = sem("key_lo")
        query_split = sem("query_split")
        value_split = sem("value_split")
        key_doubled = sem("key_doubled")
        key_stacked = sem("key_stacked")
        head_picked = sem("head_picked")
        decay_picked = sem("decay_picked")
        scores_ready = sem("scores_ready")
        max_found = sem("max_found")
        max_ready = sem("max_ready")
        exp_done = sem("exp_done")
        inverted = sem("inverted")
        prob_ready = sem("prob_ready")
        transposed = sem("transposed")
        pt_hi = sem("pt_hi")
        pt_split = sem("pt_split")
        pv_ready = sem("pv_ready")
        y_low = sem("y_low")
        y_summed = sem("y_summed")
        attn_y_hi = sem("attn_y_hi")
        attn_y_split = sem("attn_y_split")
        gained = sem("gained")
        out_psum_ready = sem("out_psum_ready")
        out_ready = (sem("out_ready_vector"), sem("out_ready_scalar"))

        UNITS = ("pool0", "pool1", "cc0", "cc1", "ch0", "ch1", "cb0", "cb1", "pm0", "pm1",
                 "v0a", "v0b", "v1a", "v1b", "f", "q0", "q1", "q2", "q3", "k0", "k1", "k2", "k3")
        SLOT = dict(zip(UNITS, (0, 1, 2, 3, 0, 1, 2, 3, 0, 1,
                                2, 3, 0, 1, 2, 3, 0, 1, 2, 3, 0, 1, 2)))
        NORM_SLOT = 3

        def done(name):
            return UNITS.index(name) + 1

        def counter(c, j):
            return lambda m, a: m * c + a + 2 * m * j

        def pair_at(base, n, j):
            return (base + n) % 2, 16 * ((base + n) // 2 + 1) + 48 * j

        block = ctx.enter_context(nc.Block())

        @block.sync
        def _(sp):
            def columns(w, col):
                return w.rearrange("(k p) f -> p k f", p=P)[:, :, bass.ds(col, PAIR)]

            def rows(w, chunk):
                return w.rearrange("(c p) d -> p c d", p=P)[:, bass.ds(chunk, 2), :]

            def load(base, n, j, src, chunks):
                slot, _ = pair_at(base, n, j)
                if base + n >= 2:
                    sp.wait_ge(weights_split, base + n - 1 + 6 * j)
                dst = raw[:, slot, :].rearrange("p (c f) -> p c f", c=chunks)
                sp.dma_start(dst, src).then_inc(raw_loaded[slot], 16)

            def swiglu(s, w_in, w_out):
                def gate_up(c, j):
                    group = counter(c, j)
                    load(N_FFN[s], gate_pair(c), j, columns(w_in, group(PAIR, 0)), KD)
                    load(N_FFN[s], gate_pair(c) + 1, j, columns(w_in, group(PAIR, F)), KD)

                def down(c, j):
                    load(N_FFN[s], down_pair(c), j, rows(w_out, counter(c, j)(2, 0)), 2)

                gate_up(0, 0)
                gate_up(1, 0)
                down(0, 0)
                with sp.Fori(0, TURNS - 1) as j:
                    for c in (1, 2):
                        gate_up(c + 1, j)
                        down(c, j)
                gate_up(GROUPS - 1, 0)
                down(GROUPS - 2, 0)
                down(GROUPS - 1, 0)

            for c in range(4):
                sp.dma_start(x_in[:, 2 * c:2 * c + 2, :],
                             x.rearrange("(c p) d -> p c d", p=P)[:, 2 * c:2 * c + 2, :])\
                    .then_inc(x_loaded[c], 16)
            swiglu(0, w1_in, w1_out)
            for n, src, chunks in (
                    (N_POOL, columns(wm_in, COL_POOL), KD), (N_CC, columns(wm_in, COL_CC), KD),
                    (N_CH, columns(wm_in, COL_CH), KD), (N_CB, columns(wm_in, COL_CB), KD),
                    (N_OUT_POOL, rows(wm_out, 4), 2),
                    (N_V0, columns(wm_in, COL_V), KD), (N_V1, columns(wm_in, COL_V + PAIR), KD),
                    (N_OUT_CONV, rows(wm_out, 6), 2),
                    (N_Q0, columns(wm_in, COL_Q), KD), (N_Q1, columns(wm_in, COL_Q + PAIR), KD),
                    (N_K0, columns(wm_in, COL_K), KD), (N_K1, columns(wm_in, COL_K + PAIR), KD),
                    (N_OUT_A0, rows(wm_out, 0), 2), (N_OUT_A1, rows(wm_out, 2), 2)):
                load(0, n, 0, src, chunks)
            swiglu(1, w2_in, w2_out)
            for c in range(NT):
                sp.wait_ge(out_ready[c % 2], c // 2 + 1)
                sp.dma_start(out[c * P:(c + 1) * P, :], x_out[:, c, :]).then_inc(out_stored, 16)
            sp.wait_ge(out_stored, 16 * NT)

        @block.gpsimd
        def _(pool):
            pool.dma_start(vec[:, :], vectors).then_inc(vec_loaded, 16)
            pool.dma_start(wf_raw[:, :, :], wm_in.rearrange("(k p) f -> p k f", p=P)
                           [:, :, COL_F:COL_F + HEADS]).then_inc(wf_loaded, 16)
            pool.memset(ones2[:, :], 1.0)
            pool.memset(tri[:, :], 0.0)
            pool.memset(ident[:, :], 0.0).then_inc(consts_cleared, 1)
            pool.wait_ge(consts_cleared, 1)
            pool.affine_select(out=ident[:, :], in_=ident[:, :], compare_op=ALU.not_equal, fill=1.0,
                               base=0, pattern=[[-1, P]], channel_multiplier=1)
            pool.affine_select(out=tri[:, :], in_=tri[:, :], compare_op=ALU.is_ge, fill=MASKED,
                               base=0, pattern=[[-1, P]], channel_multiplier=1)\
                .then_inc(consts_ready, 1)
            pool.wait_ge(r_rows_ready, 2)
            pool.memset(wp_raw[:, :, :], 0.0).then_inc(wp_cleared, 1)
            pool.wait_ge(wp_cleared, 1)
            for g in range(len(WINDOWS)):
                h = (g % 2) * HD
                pool.dma_start(wp_raw[h:h + HD, g // 2, h:h + HD], w_pool[g, :, :])\
                    .then_inc(wp_loaded, 16)

            pool.wait_ge(mask_ready, 1)
            pool.wait_ge(decay_ready, 1)
            for h in range(HEADS):
                b = h % 2
                own, other = halves(b)
                if h > 0:
                    pool.wait_ge(key_stacked, h)
                pool.tensor_copy(head_col[:, :], head_mask[:, h:h + 1]).then_inc(head_picked, 1)
                pool.wait_ge(head_picked, h + 1)
                if h >= 2:
                    pool.wait_ge(scores_ready, NT * (h - 1))
                pool.tensor_scalar(decay_h[:, b, :], f32(decay_k[:, :]), head_col[:, 0:1], None,
                                   ALU.mult).then_inc(decay_picked, 1)
                pool.wait_ge(decay_picked, h + 1)
                pool.wait_ge(key_hi, h + 1)
                pool.tensor_copy(k_hi[other, b, :], f32(k_hi[own, b, :])).then_inc(key_doubled, 1)
                pool.wait_ge(key_doubled, h + 1)
                pool.wait_ge(key_lo, h + 1)
                pool.tensor_copy(k_lo[other, b, :], f32(k_lo[own, b, :])).then_inc(key_stacked, 1)

        @block.scalar
        def _(act):
            def copy(dst, src, scale=1.0):
                return act.activation(dst, src, ACT.Copy, scale=scale)

            def split_hi(w, base, n, j=0):
                slot, loaded = pair_at(base, n, j)
                act.wait_ge(raw_loaded[slot], loaded)
                copy(flat(w, HI), raw[:, slot, :]).then_inc(weights_hi, 1)

            def gain_hi(k, v):
                act.activation(xg[:, HI, k, :], xt[:, k, :], ACT.Identity,
                               scale=vec[:, v + k:v + k + 1]).then_inc(xg_hi, 1)

            def square(s, k):
                if k >= 2:
                    act.wait_ge(sumsq_added, (KD - 1) * (s - 1) + k - 1)
                act.activation(tmp[:, min(k, 1), :], xt[:, k, :], ACT.Square)\
                    .then_inc(square_ready, 1)

            def gain_and_square(s, before, v):
                for k in range(KD):
                    act.wait_ge(x_updated, before + k + 1)
                    gain_hi(k, v)
                    square(s, k)

            def root_step(s):
                act.wait_ge(ms_ready, s + 1)
                act.activation(root[:, :], ms[:, :], ACT.Sqrt).then_inc(root_ready, 1)

            def swiglu(s):
                base, g0, x0 = N_FFN[s], 2 * GROUPS * s, X_BASE[s]

                def hidden(c, j):
                    i = counter(c, j)
                    for f in range(2):
                        act.wait_ge(gate_scaled, i(2, g0 + f + 1))
                        act.activation(tmp[:, 1, :], tmp[:, 0, :], ACT.Sigmoid)\
                            .then_inc(sigmoid_ready, 1)
                        if f == 0 and c > 0:
                            act.wait_ge(x_psum_ready, i(KD, x0 - KD))
                        act.wait_ge(hidden_ready, i(2, g0 + f + 1))
                        copy(hid[c % 2][:, HI, f, :], tmp[:, 0, :]).then_inc(hidden_hi, 1)

                def split_gate_up(c, j):
                    i = counter(c, j)
                    act.wait_ge(gate_ready, i(2, g0))
                    split_hi(w_a, base, gate_pair(c), j)
                    act.wait_ge(up_ready, i(2, g0))
                    split_hi(w_b, base, gate_pair(c) + 1, j)

                def split_down(c, j):
                    act.wait_ge(x_psum_ready, counter(c, j)(KD, x0))
                    split_hi(w_o, base, down_pair(c), j)

                hidden(0, 0)
                split_gate_up(1, 0)
                split_down(0, 0)
                with act.Fori(0, TURNS - 1) as j:
                    for c in (1, 2):
                        hidden(c, j)
                        split_gate_up(c + 1, j)
                        split_down(c, j)
                hidden(GROUPS - 2, 0)
                split_gate_up(GROUPS - 1, 0)
                split_down(GROUPS - 2, 0)
                hidden(GROUPS - 1, 0)
                split_down(GROUPS - 1, 0)

            act.wait_ge(consts_ready, 1)
            copy(ident_r[:, :], ident[:, :])
            copy(causal_r[:, :], tri[:, :]).then_inc(consts_rounded, 1)
            act.wait_ge(vec_loaded, 16)
            for c in range(NT):
                if c % 2 == 0:
                    act.wait_ge(x_loaded[c // 2], 16)
                act.activation(x_squares[:, c, :], x_in[:, c, :], ACT.Square,
                               accum_out=sums_x[:, c:c + 1]).then_inc(input_squared, 1)
            for k in range(KD):
                act.wait_ge(x_updated, k + 1)
                gain_hi(k, V_NORM1)
            act.wait_ge(input_squared, NT)
            split_hi(w_a, 0, 0)
            split_hi(w_b, 0, 1)
            root_step(0)
            swiglu(0)

            act.wait_ge(gate_ready, 2 * GROUPS)
            split_hi(w_a, 0, N_POOL)
            act.wait_ge(up_ready, 2 * GROUPS)
            split_hi(w_b, 0, N_CC)
            gain_and_square(1, X_MIX - KD, V_MIX)
            root_step(1)
            act.wait_ge(proj_ready, done("pool1"))
            split_hi(w_a, 0, N_CH)
            act.wait_ge(wp_loaded, 16 * len(WINDOWS))
            copy(wp_r[:, HI, :, :], wp_raw[:, :, :]).then_inc(wp_hi, 1)
            for c in range(2):
                act.wait_ge(pooled_ready, c + 1)
                copy(hid0[:, HI, c, :], pool_u).then_inc(pooled_hi, 1)
            act.wait_ge(proj_ready, done("cc1"))
            split_hi(w_b, 0, N_CB)
            act.wait_ge(x_psum_ready, X_MIX)
            split_hi(w_o, 0, N_OUT_POOL)
            act.wait_ge(proj_ready, done("ch1"))
            split_hi(w_a, 0, N_V0)
            act.wait_ge(proj_ready, done("cb1"))
            split_hi(w_b, 0, N_V1)
            for c in range(2):
                act.wait_ge(proj_ready, done("pm%d" % c))
                act.activation(hid0[:, HI, c, :], unit(SLOT["pm%d" % c]), ACT.Identity,
                               scale=vec[:, V_PSCALE + c:V_PSCALE + c + 1]).then_inc(pool_y_hi, 1)
            act.wait_ge(x_psum_ready, X_MIX + KD)
            act.wait_ge(conv_y_ready, 2)
            for c in range(2):
                copy(hid0[:, HI, c, :], conv_cc[:, c, :]).then_inc(conv_y_hi, 1)
            split_hi(w_o, 0, N_OUT_CONV)
            act.wait_ge(proj_ready, done("v0b"))
            act.wait_ge(wf_loaded, 16)
            copy(wf[:, :, 0:HEADS], wf_raw[:, :, :]).then_inc(wf_hi, 1)
            act.wait_ge(proj_ready, done("v1b"))
            split_hi(w_b, 0, N_Q0)
            act.wait_ge(proj_ready, done("f"))
            copy(row(0, 0), unit(SLOT["f"])[32:32 + HEADS, :]).then_inc(forget_low, 1)
            split_hi(w_a, 0, N_Q1)
            act.wait_ge(forget_abs, 1)
            act.activation(row(0, 1), row(0, 0), ACT.Exp, scale=-1.0).then_inc(forget_exp, 1)
            act.wait_ge(forget_sum, 1)
            act.activation(row(0, 2), row(1, 1), ACT.Ln).then_inc(forget_log, 1)
            act.wait_ge(forget_log, 1)
            act.wait_ge(forget_lost, 1)
            act.activation(row(0, 1), row(0, 2), ACT.Exp, scale=-1.0).then_inc(forget_inv, 1)
            act.wait_ge(proj_ready, done("q1"))
            split_hi(w_b, 0, N_K0)
            act.wait_ge(proj_ready, done("q3"))
            split_hi(w_a, 0, N_K1)

            act.wait_ge(decay_filled, 1)
            act.wait_ge(decay_summed, 1)
            copy(decay_k[0:HEADS, :], row(1, 0), 1 / SCALE).then_inc(decay_hi, 1)
            act.wait_ge(decay_hi, 1)
            copy(decay_q[64:64 + HEADS, :], f32(decay_k[0:HEADS, :]), -1.0)
            act.wait_ge(decay_lo, 1)
            copy(decay_q[96:96 + HEADS, :], f32(decay_k[32:32 + HEADS, :]), -1.0)\
                .then_inc(decay_ready, 1)
            act.wait_ge(proj_taken, done("k3"))

            def keys(h, j):
                own, _ = halves(h % 2)
                if h >= 2:
                    act.wait_ge(pv_ready, groups_done(HEAD_GROUPS * (h - 1) - 1, j))
                copy(k_hi[own, h % 2, :], of_pair(k_plain, own, h, j)).then_inc(key_hi, 1)

            def queries(h, j):
                own, _ = halves(h % 2)
                copy(q_st[own, h % 2, :], of_pair(q_plain, own, h, j)).then_inc(query_hi, 1)

            def values(h, j):
                copy(v_st[:, h % 2, :, 0:HD], v_of(h, j)).then_inc(value_hi, 1)

            def iteration(t, j):
                if LAG <= t < STEPS + LAG:
                    r = t - LAG
                    to = P * (r % 2)
                    act.wait_ge(transposed, steps_done(r, j))
                    if r % 2 == 0 and r >= 2:
                        act.wait_ge(pv_ready, groups_done(r // 2 - 1, j))
                    for _, part in pt_banks(r):
                        copy(pt[:, HI, part, to:to + P], chunks_in_psum(part)).then_inc(pt_hi, 1)
                if t >= 5 and t % 2 == 1 and (t - 5) // 2 < STEPS // 2:
                    g = (t - 5) // 2
                    act.wait_ge(pv_ready, groups_done(g, j))
                    if g > 0 and g % TURN_GROUPS in (0, HEAD_GROUPS // 2):
                        before = 2 * (g // TURN_GROUPS) - 1 + g % TURN_GROUPS // 2
                        if before > 0:
                            act.wait_ge(attn_y_split, before + 2 * j)
                    copy(y_of(g), ps[HD:2 * HD, 6 + g % 2, 0:QG]).then_inc(y_low, 1)
                if t < STEPS:
                    s, n = t % 2, P * (t % NT + 1)
                    if t >= PROBS:
                        act.wait_ge(transposed, steps_done(t - PROBS, j))
                    act.wait_ge(max_ready, steps_done(t, j))
                    act.activation(prob[:, t % PROBS, 0:n], unit(s)[:, 0:n], ACT.Exp,
                                   bias=exp_bias[:, s:s + 1], scale=SCALE,
                                   accum_out=exp_sum[:, t % PROBS:t % PROBS + 1])\
                        .then_inc(exp_done, 1)
                if t >= TURN and t % TURN in Y_HI_AT:
                    pair, half = t // TURN - 1, Y_HI_AT.index(t % TURN)
                    last = HEAD_GROUPS + HEAD_GROUPS // 2 * (half + 1) - 1
                    cols = slice(half * BANK, (half + 1) * BANK)
                    act.wait_ge(y_summed, groups_done(TURN_GROUPS * pair + last, j))
                    copy(y_hi[:, bass.ds(pair + j, 1), cols].rearrange("p a t -> p (a t)"),
                         y_f[:, cols]).then_inc(attn_y_hi, 1)
                for offset, stage in ((4, keys), (5, queries), (NT, values)):
                    h = blocks(t, offset)
                    if h is not None:
                        stage(h, j)
                if t == STEPS - 5:
                    split_hi(out_w[0], 0, N_OUT_A0)
                if t == STEPS - 4:
                    act.wait_ge(value_split, HEADS)
                    split_hi(out_w[1], 0, N_OUT_A1)

            keys(0, 0)
            queries(0, 0)
            pipeline(act, iteration)

            act.wait_ge(transposed, STEPS)
            split_hi(w_a, N_FFN[1], 0)
            gain_and_square(2, X_FFN2 - KD, V_NORM2)
            act.wait_ge(x_psum_ready, X_FFN2)
            split_hi(w_b, N_FFN[1], 1)
            root_step(2)
            swiglu(1)
            act.wait_ge(up_ready, 4 * GROUPS)
            for k in range(KD):
                act.wait_ge(x_updated, X_END - KD + k + 1)
                square(3, k)
                act.activation(x_gain[:, k, :], xt[:, k, :], ACT.Identity,
                               scale=vec[:, V_FINAL + k:V_FINAL + k + 1]).then_inc(gained, 1)
            root_step(3)
            act.wait_ge(r_col_ready, 4)
            for c in range(1, NT, 2):
                act.wait_ge(out_psum_ready, c + 1)
                act.activation(x_out[:, c, :], unit(c % 4), ACT.Identity,
                               scale=r_col[:, c:c + 1]).then_inc(out_ready[1], 1)

        @block.vector
        def _(dve):
            steps = [0]

            def link(ins):
                steps[0] += 1
                ins.then_inc(chain, 1)
                dve.wait_ge(chain, steps[0])

            def mul(dst, a, b):
                return dve.tensor_tensor(out=dst, in0=a, in1=b, op=ALU.mult)

            def add(dst, a, b):
                return dve.tensor_tensor(out=dst, in0=a, in1=b, op=ALU.add)

            def lo_part(dst, value, hi):
                return dve.tensor_tensor(out=dst, in0=value, in1=f32(hi), op=ALU.subtract)

            def scaled_lo(dst, value, scale, hi):
                return dve.scalar_tensor_tensor(out=dst, in0=value, scalar=scale, in1=f32(hi),
                                                op0=ALU.mult, op1=ALU.subtract)

            def split_lo(w, base, n, j=0):
                slot, _ = pair_at(base, n, j)
                dve.wait_ge(weights_hi, base + n + 1 + 6 * j)
                lo_part(flat(w, LO), raw[:, slot, :], flat(w, HI)).then_inc(weights_split, 1)

            def gain_lo(s, k, v):
                dve.wait_ge(xg_hi, KD * s + k + 1)
                scaled_lo(xg[:, LO, k, :], xt[:, k, :], vec[:, v + k:v + k + 1], xg[:, HI, k, :])\
                    .then_inc(xg_split, 1)

            def residual(k, factor, at_count, last_count, cols=slice(0, T), psum=None):
                dve.wait_ge(x_psum_ready, at_count)
                dve.wait_ge(x_updated, last_count)
                dve.scalar_tensor_tensor(out=xt[:, k, cols], in0=psum, scalar=factor,
                                         in1=xt[:, k, cols], op0=ALU.mult, op1=ALU.add)\
                    .then_inc(x_updated, 1)

            def sum_square(s, k):
                dve.wait_ge(square_ready, KD * (s - 1) + k + 1)
                if k >= 2:
                    dve.wait_ge(sumsq_added, (KD - 1) * (s - 1) + k - 1)
                add(tmp[:, 0, :], tmp[:, 0, :], tmp[:, 1, :]).then_inc(sumsq_added, 1)

            def inverse_rms(s):
                if s == 0:
                    dve.wait_ge(input_squared, NT)
                    sums = sums_x[:, :]
                else:
                    dve.wait_ge(r_sum_ready, s)
                    sums = ps[:, 2 * NORM_SLOT, 0:2 * NT]\
                        .rearrange("p (c two) -> p c two", two=2)[:, :, 0]
                dve.tensor_scalar(ms[:, :], sums, 1.0 / D, EPS, ALU.mult, ALU.add)\
                    .then_inc(ms_ready, 1)
                dve.wait_ge(root_ready, s + 1)
                link(dve.reciprocal(root[:, :], root[:, :]))
                link(mul(newton[:, :], root[:, :], root[:, :]))
                link(mul(newton[:, :], newton[:, :], ms[:, :]))
                link(dve.tensor_scalar(newton[:, :], newton[:, :], -0.5, 1.5, ALU.mult, ALU.add))
                mul(r_col[:, :], root[:, :], newton[:, :]).then_inc(r_col_ready, 1)

            def spread_rms(s):
                dve.wait_ge(r_bcast_ready, s + 1)
                dve.tensor_copy(r_rows[:, :], unit(NORM_SLOT)).then_inc(r_rows_ready, 1)
                dve.wait_ge(r_rows_ready, s + 1)

            def split_and_sum(s, v, update):
                for k in range(KD + 1):
                    if k < KD:
                        update(k)
                    if k > 0:
                        gain_lo(s, k - 1, v)
                    if k > 1:
                        sum_square(s, k - 1)

            def norm(s):
                inverse_rms(s)
                spread_rms(s)

            def swiglu(s, tail):
                base, g0, x0 = N_FFN[s], 2 * GROUPS * s, X_BASE[s]

                def hidden(c, j):
                    i = counter(c, j)
                    for f in range(2):
                        now = i(2, g0 + f + 1)
                        dve.wait_ge(gate_ready, now)
                        if c > 0 or f > 0:
                            dve.wait_ge(hidden_split, now - 1)
                        mul(tmp[:, 0, :], unit(2 * f), r_rows[:, :]).then_inc(gate_scaled, 1)
                        dve.wait_ge(sigmoid_ready, now)
                        mul(tmp[:, 0, :], tmp[:, 0, :], tmp[:, 1, :]).then_inc(gated, 1)
                        dve.wait_ge(gated, now)
                        dve.wait_ge(up_ready, now)
                        mul(tmp[:, 1, :], unit(2 * f + 1), r_rows[:, :]).then_inc(up_scaled, 1)
                        dve.wait_ge(up_scaled, now)
                        mul(tmp[:, 0, :], tmp[:, 0, :], tmp[:, 1, :]).then_inc(hidden_ready, 1)
                        dve.wait_ge(hidden_hi, now)
                        lo_part(hid[c % 2][:, LO, f, :], tmp[:, 0, :], hid[c % 2][:, HI, f, :])\
                            .then_inc(hidden_split, 1)

                def update(c, j, k):
                    i = counter(c, j)
                    residual(k, 0.5, i(KD, x0 + k + 1), i(KD, x0 + k + 1 - KD), psum=unit(k % 4))

                def split_gate(c, j):
                    split_lo(w_a, base, gate_pair(c), j)

                def split_up(c, j):
                    split_lo(w_b, base, gate_pair(c) + 1, j)

                def split_down(c, j):
                    split_lo(w_o, base, down_pair(c), j)

                def step(c, j, more):
                    hidden(c, j)
                    for k in range(KD):
                        update(c - 1, j, k)
                        if more and k == 1:
                            split_gate(c + 1, j)
                        if more and k == 3:
                            split_up(c + 1, j)
                    split_down(c, j)

                hidden(0, 0)
                split_gate(1, 0)
                split_up(1, 0)
                split_down(0, 0)
                with dve.Fori(0, TURNS - 1) as j:
                    step(1, j, True)
                    step(2, j, True)
                step(GROUPS - 2, 0, True)
                step(GROUPS - 1, 0, False)
                tail(lambda k: update(GROUPS - 1, 0, k))

            dve.wait_ge(consts_ready, 1)
            dve.tensor_reduce(head_mask[:, :], ident[:, :].rearrange("p (q h) -> p h q", q=4)
                              [:, 0:HEADS, :], AX.X, ALU.add).then_inc(mask_ready, 1)
            dve.wait_ge(vec_loaded, 16)
            for k in range(KD + 1):
                if k < KD:
                    dve.wait_ge(x_psum_ready, k + 1)
                    dve.tensor_copy(xt[:, k, :], unit(k % 4)).then_inc(x_updated, 1)
                if k > 0:
                    dve.wait_ge(x_updated, k)
                    gain_lo(0, k - 1, V_NORM1)
            split_lo(w_a, 0, 0)
            split_lo(w_b, 0, 1)
            norm(0)

            def before_mixer(update):
                split_lo(w_a, 0, N_POOL)
                split_lo(w_b, 0, N_CC)
                split_and_sum(1, V_MIX, update)
                norm(1)

            swiglu(0, before_mixer)

            def take(name, dst):
                dve.wait_ge(proj_ready, done(name))
                return mul(dst, unit(SLOT[name]), r_rows[:, :])

            def taken_and_linked(name, ins):
                ins.then_inc(proj_taken, 1)
                dve.wait_ge(proj_taken, done(name))

            def window(dst, src, shift, rows=slice(0, P)):
                link(add(dst[rows, WMAX:], src[rows, WMAX:], src[rows, WMAX - shift:T + WMAX - shift]))

            upper = slice(HD, P)
            dve.memset(pool_a[:, 0:WMAX], 0.0)
            link(dve.memset(pool_b[:, 0:WMAX], 0.0))
            for c in range(2):
                if c > 0:
                    dve.wait_ge(pooled_split, c)
                taken_and_linked("pool%d" % c, take("pool%d" % c, pool_u))
                add(pool_a[:, WMAX + 1:], pool_u[:, 1:], pool_u[:, 0:T - 1])
                link(dve.tensor_copy(pool_a[:, WMAX:WMAX + 1], pool_u[:, 0:1]))
                if c == 0:
                    window(pool_b, pool_a, 2, upper)
                else:
                    window(pool_b, pool_a, 2)
                    window(pool_a, pool_b, 4)
                    window(pool_b, pool_a, 8, upper)
                counts = vec[:, V_COUNT + c * WMAX:V_COUNT + (c + 1) * WMAX]
                for rows, sums in ((slice(0, HD), pool_a), (upper, pool_b)):
                    dve.scalar_tensor_tensor(
                        out=pool_u[rows, WMAX:], in0=sums[rows, 2 * WMAX:],
                        scalar=counts[rows, WMAX - 1:WMAX], in1=pool_u[rows, WMAX:],
                        op0=ALU.mult, op1=ALU.subtract)
                    link(mul(sums[rows, WMAX:2 * WMAX], sums[rows, WMAX:2 * WMAX], counts[rows, :]))
                    last = dve.tensor_tensor(out=pool_u[rows, 0:WMAX], in0=sums[rows, WMAX:2 * WMAX],
                                             in1=pool_u[rows, 0:WMAX], op=ALU.subtract)
                last.then_inc(pooled_ready, 1)
                dve.wait_ge(pooled_hi, c + 1)
                lo_part(hid0[:, LO, c, :], pool_u, hid0[:, HI, c, :]).then_inc(pooled_split, 1)
                if c == 0:
                    dve.wait_ge(wp_hi, 1)
                    lo_part(wp_r[:, LO, :, :], wp_raw[:, :, :], wp_r[:, HI, :, :])\
                        .then_inc(wp_split, 1)
            split_lo(w_a, 0, N_CH)

            dve.wait_ge(pooled_split, 2)
            link(dve.memset(conv_u[:, :, 0:TAPS - 1], 0.0))
            for c in range(2):
                name = "cc%d" % c
                taken_and_linked(name, take(name, conv_cc[:, c, :]))
            split_lo(w_b, 0, N_CB)
            split_lo(w_o, 0, N_OUT_POOL)
            for c in range(2):
                name = "ch%d" % c
                u, y = conv_u[:, c, :], conv_cc[:, c, :]
                taken_and_linked(name, take(name, u[:, TAPS - 1:]))
                link(mul(u[:, TAPS - 1:], u[:, TAPS - 1:], y))
                tap = [vec[:, V_CONV + c * TAPS + w:V_CONV + c * TAPS + w + 1] for w in range(TAPS)]
                link(dve.tensor_scalar(y, u[:, TAPS - 1:], tap[TAPS - 1], None, ALU.mult))
                for w in range(TAPS - 1):
                    link(dve.scalar_tensor_tensor(out=y, in0=u[:, w:w + T], scalar=tap[w], in1=y,
                                                  op0=ALU.mult, op1=ALU.add))
            split_lo(w_a, 0, N_V0)
            for c in range(2):
                name = "cb%d" % c
                if c > 0:
                    dve.wait_ge(conv_y_ready, c)
                taken_and_linked(name, take(name, conv_b))
                mul(conv_cc[:, c, :], conv_cc[:, c, :], conv_b).then_inc(conv_y_ready, 1)
            split_lo(w_b, 0, N_V1)

            for c in range(2):
                name = "pm%d" % c
                dve.wait_ge(pool_y_hi, c + 1)
                scaled_lo(hid0[:, LO, c, :], unit(SLOT[name]),
                          vec[:, V_PSCALE + c:V_PSCALE + c + 1], hid0[:, HI, c, :])\
                    .then_inc(proj_taken, 1)
            for k in range(KD):
                now = X_MIX + k + 1
                residual(k, 1.0, now, now - KD, psum=unit((2 + k) % 4))
            for c in range(2):
                dve.wait_ge(conv_y_hi, c + 1)
                lo_part(hid0[:, LO, c, :], conv_cc[:, c, :], hid0[:, HI, c, :])\
                    .then_inc(conv_y_split, 1)
            split_lo(w_o, 0, N_OUT_CONV)
            dve.wait_ge(conv_y_split, 2)

            for n, name in enumerate(("v0a", "v0b", "v1a", "v1b")):
                dve.wait_ge(proj_ready, done(name))
                for i in range(4):
                    c = 4 * (n % 2) + i
                    last = dve.tensor_scalar(
                        v_plain[:, c, PAIR * (n // 2):PAIR * (n // 2 + 1)],
                        unit(SLOT[name])[:, i * PAIR:(i + 1) * PAIR], r_col[:, c:c + 1], None,
                        ALU.mult)
                last.then_inc(proj_taken, 1)
                if n == 1:
                    dve.wait_ge(wf_hi, 1)
                    lo_part(wf[:, :, 32:32 + HEADS], wf_raw[:, :, :], wf[:, :, 0:HEADS])\
                        .then_inc(wf_split, 1)
            split_lo(w_b, 0, N_Q0)

            dve.wait_ge(forget_low, 1)
            add(row(1, 0), unit(SLOT["f"])[0:HEADS, :], row(0, 0)).then_inc(proj_taken, 1)
            dve.wait_ge(proj_taken, done("f"))
            link(mul(row(1, 0), row(1, 0), r_rows[0:HEADS, :]))
            link(dve.tensor_scalar(row(1, 0), row(1, 0), vec[0:HEADS, V_BFORGET:V_BFORGET + 1],
                                   None, ALU.add))
            dve.scalar_tensor_tensor(out=row(0, 0), in0=row(1, 0), scalar=-1.0, in1=row(1, 0),
                                     op0=ALU.mult, op1=ALU.max).then_inc(forget_abs, 1)
            split_lo(w_a, 0, N_Q1)
            dve.wait_ge(forget_exp, 1)
            dve.tensor_scalar(row(1, 1), row(0, 1), 1.0, None, ALU.add).then_inc(forget_sum, 1)
            dve.wait_ge(forget_log, 1)
            dve.scalar_tensor_tensor(out=row(1, 1), in0=row(1, 1), scalar=-1.0, in1=row(0, 1),
                                     op0=ALU.add, op1=ALU.subtract).then_inc(forget_lost, 1)
            dve.wait_ge(forget_inv, 1)
            link(mul(row(1, 2), row(1, 1), row(0, 1)))
            link(dve.tensor_tensor(out=row(0, 2), in0=row(0, 2), in1=row(1, 2), op=ALU.subtract))
            link(dve.tensor_scalar(row(1, 2), row(1, 0), -1.0, 0.0, ALU.mult, ALU.max))
            dve.tensor_tensor_scan(row(1, 0), row(1, 2), row(0, 2), 0.0, ALU.add, ALU.add)\
                .then_inc(decay_summed, 1)

            for k in range(KD):
                now = X_MIX + KD + k + 1
                residual(k, 1.0, now, now - KD, psum=unit((3 + k) % 4))
            for n, (part, pair) in enumerate(((q_plain, 0), (q_plain, 2), (k_plain, 0), (k_plain, 2))):
                for i in range(2):
                    name = ("q%d" if part is q_plain else "k%d") % (pair + i)
                    take(name, part[:, pair + i, :]).then_inc(proj_taken, 1)
                if n == 0:
                    split_lo(w_b, 0, N_K0)
                if n == 1:
                    split_lo(w_a, 0, N_K1)

            dve.memset(f32(decay_k[:, :]), 1.0)
            dve.memset(f32(decay_q[:, :]), 1.0).then_inc(decay_filled, 1)
            dve.wait_ge(decay_summed, 1)
            dve.wait_ge(decay_hi, 1)
            scaled_lo(decay_k[32:32 + HEADS, :], row(1, 0), 1 / SCALE, decay_k[0:HEADS, :])\
                .then_inc(decay_lo, 1)
            dve.wait_ge(proj_taken, done("k3"))

            def keys(h, j):
                own, _ = halves(h % 2)
                dve.wait_ge(key_hi, heads_done(h, j))
                lo_part(k_lo[own, h % 2, :], of_pair(k_plain, own, h, j), k_hi[own, h % 2, :])\
                    .then_inc(key_lo, 1)

            def queries(h, j):
                own, other = halves(h % 2)
                dve.wait_ge(query_hi, heads_done(h, j))
                lo_part(q_st[other, h % 2, :], of_pair(q_plain, own, h, j), q_st[own, h % 2, :])\
                    .then_inc(query_split, 1)

            def values(h, j):
                dve.wait_ge(value_hi, heads_done(h, j))
                lo_part(v_st[:, h % 2, :, HD:2 * HD], v_of(h, j), v_st[:, h % 2, :, 0:HD])\
                    .then_inc(value_split, 1)

            def iteration(t, j):
                if t >= 6 and t % 2 == 0 and (t - 6) // 2 < STEPS // 2:
                    g = (t - 6) // 2
                    dve.wait_ge(y_low, groups_done(g, j))
                    add(y_of(g), ps[0:HD, 6 + g % 2, 0:QG], y_of(g)).then_inc(y_summed, 1)
                if LAG <= t < STEPS + LAG:
                    r = t - LAG
                    to = P * (r % 2)
                    for bank, part in pt_banks(r):
                        dve.wait_ge(pt_hi, banks_done(r, j, bank))
                        lo_part(pt[:, LO, part, to:to + P], chunks_in_psum(part),
                                pt[:, HI, part, to:to + P]).then_inc(pt_split, 1)
                if 1 <= t < STEPS + 1:
                    r = t - 1
                    i = r % PROBS
                    dve.wait_ge(exp_done, steps_done(r, j))
                    dve.reciprocal(exp_inv[:, i:i + 1], exp_sum[:, i:i + 1]).then_inc(inverted, 1)
                    dve.wait_ge(inverted, steps_done(r, j))
                    probs = prob[:, i, 0:P * (r % NT + 1)]
                    dve.tensor_scalar(probs, probs, exp_inv[:, i:i + 1], None, ALU.mult)\
                        .then_inc(prob_ready, 1)
                if t < STEPS:
                    s, n = t % 2, P * (t % NT + 1)
                    dve.wait_ge(scores_ready, steps_done(t, j))
                    dve.tensor_reduce(row_max[:, s:s + 1], unit(s)[:, 0:n], AX.X, ALU.max)\
                        .then_inc(max_found, 1)
                    dve.wait_ge(max_found, steps_done(t, j))
                    dve.tensor_scalar(exp_bias[:, s:s + 1], row_max[:, s:s + 1], -SCALE, None,
                                      ALU.mult).then_inc(max_ready, 1)
                for offset, stage in ((5, keys), (6, queries), (NT + 1, values)):
                    h = blocks(t, offset)
                    if h is not None:
                        stage(h, j)
                if t >= TURN and t % TURN in Y_LO_AT:
                    pair, half = t // TURN - 1, Y_LO_AT.index(t % TURN)
                    cols = slice(half * BANK, (half + 1) * BANK)
                    at_pair = bass.ds(pair + j, 1)
                    dve.wait_ge(attn_y_hi, 2 * pair + half + 1 + 2 * j)
                    lo_part(y_lo[:, at_pair, cols].rearrange("p a t -> p (a t)"), y_f[:, cols],
                            y_hi[:, at_pair, cols].rearrange("p a t -> p (a t)"))\
                        .then_inc(attn_y_split, 1)
                if t == STEPS - 4:
                    split_lo(out_w[0], 0, N_OUT_A0)
                if t == STEPS - 3:
                    split_lo(out_w[1], 0, N_OUT_A1)

            keys(0, 0)
            queries(0, 0)
            pipeline(dve, iteration)

            split_lo(w_a, N_FFN[1], 0)
            split_and_sum(2, V_NORM2, lambda k: residual(k, 1.0, X_ATTN + k + 1, X_ATTN + k + 1 - KD,
                                                         psum=unit(k % 4)))
            split_lo(w_b, N_FFN[1], 1)
            norm(2)

            def before_output(update):
                for k in range(KD + 1):
                    if k < KD:
                        update(k)
                    if k > 1:
                        sum_square(3, k - 1)
                inverse_rms(3)

            swiglu(1, before_output)
            dve.wait_ge(r_col_ready, 4)
            for c in range(0, NT, 2):
                dve.wait_ge(out_psum_ready, c + 1)
                dve.tensor_scalar(x_out[:, c, :], unit(c % 4), r_col[:, c:c + 1], None, ALU.mult)\
                    .then_inc(out_ready[0], 1)

        @block.tensor
        def _(pe):
            def projection(slot, w, chunk, ready):
                for half in range(2):
                    for k in range(KD):
                        for a, b in PASSES:
                            last = pe.matmul(ps[:, 2 * slot + half, :],
                                             w[:, a, k, chunk * P:(chunk + 1) * P],
                                             xg[:, b, k, half * BANK:(half + 1) * BANK],
                                             start=(k == 0 and (a, b) == PASSES[0]),
                                             stop=(k == KD - 1 and (a, b) == PASSES[-1]))
                last.then_inc(ready, 1)

            def output(bank, w, y, k, half):
                for f in range(2):
                    for a, b in PASSES:
                        last = pe.matmul(ps[:, bank, :], w[:, a, f, k * P:(k + 1) * P],
                                         y[:, b, f, half * BANK:(half + 1) * BANK],
                                         start=(f == 0 and (a, b) == PASSES[0]),
                                         stop=(f == 1 and (a, b) == PASSES[-1]))
                return last

            def sum_rows(s):
                pe.wait_ge(sumsq_added, (KD - 1) * s)
                for c in range(NT):
                    last = pe.matmul(ps[:, 2 * NORM_SLOT, 2 * c:2 * c + 2],
                                     tmp[:, 0, c * P:(c + 1) * P], ones2[:, :],
                                     start=True, stop=True)
                last.then_inc(r_sum_ready, 1)

            def spread_rows(s):
                pe.wait_ge(r_col_ready, s + 1)
                for c in range(NT):
                    last = pe.matmul(ps[:, 2 * NORM_SLOT + c // 4, c % 4 * P:(c % 4 + 1) * P],
                                     r_col[:, c:c + 1].to_broadcast([P, P]), ident[:, :],
                                     start=True, stop=True)
                last.then_inc(r_bcast_ready, 1)

            def swiglu(s):
                base, g0, x0 = N_FFN[s], 2 * GROUPS * s, X_BASE[s]

                def hidden(c, j):
                    i = counter(c, j)
                    for f in range(2):
                        if f == 0:
                            pe.wait_ge(weights_split, base + gate_pair(c) + 1 + 6 * j)
                        if c > 0:
                            pe.wait_ge(x_updated, i(KD, x0 - 2 * KD + 5 + 2 * f))
                            pe.wait_ge(gate_scaled, i(2, g0 + f - 1))
                        projection(2 * f, w_a, f, gate_ready)
                        if c == 0 and f == 1:
                            spread_rows(2 * s)
                            pe.wait_ge(r_rows_ready, 2 * s + 1)
                        if f == 0:
                            pe.wait_ge(weights_split, base + gate_pair(c) + 2 + 6 * j)
                        if c > 0:
                            pe.wait_ge(x_updated, i(KD, x0 - 2 * KD + 6 + 2 * f))
                            pe.wait_ge(up_scaled, i(2, g0 + f - 1))
                        projection(2 * f + 1, w_b, f, up_ready)
                        if c == 0 and f == 0 and s > 0:
                            sum_rows(2 * s)

                def down(c, j, last_group=False):
                    i = counter(c, j)
                    pe.wait_ge(weights_split, base + down_pair(c) + 1 + 6 * j)
                    pe.wait_ge(hidden_split, i(2, g0 + 2))
                    for k in range(KD):
                        if k >= 4 or last_group:
                            pe.wait_ge(x_updated, i(KD, x0 + k - 3))
                        else:
                            pe.wait_ge((gate_scaled, up_scaled)[k % 2], i(2, g0 + 3 + k // 2))
                        for half in range(2):
                            last = output(2 * (k % 4) + half, w_o, hid[c % 2], k, half)
                        last.then_inc(x_psum_ready, 1)

                pe.wait_ge(xg_split, KD * (2 * s + 1))
                hidden(0, 0)
                with pe.Fori(0, TURNS) as j:
                    hidden(1, j)
                    down(0, j)
                    hidden(2, j)
                    down(1, j)
                down(GROUPS - 1, 0, True)

            pe.wait_ge(consts_ready, 1)
            for c in range(4):
                pe.wait_ge(x_loaded[c], 16)
            for k in range(KD):
                if k >= 4:
                    pe.wait_ge(x_updated, k - 3)
                for c in range(NT):
                    last = pe.transpose(unit(k % 4)[:, c * P:(c + 1) * P],
                                        x_in[:, c, k * P:(k + 1) * P], ident[:, :])
                last.then_inc(x_psum_ready, 1)
            swiglu(0)

            pe.wait_ge(xg_split, 2 * KD)
            pe.wait_ge(weights_split, N_POOL + 1)
            projection(0, w_a, 0, proj_ready)
            projection(1, w_a, 1, proj_ready)
            sum_rows(1)
            pe.wait_ge(weights_split, N_CC + 1)
            projection(2, w_b, 0, proj_ready)
            spread_rows(1)
            pe.wait_ge(r_rows_ready, 2)
            projection(3, w_b, 1, proj_ready)

            def pair(w, n, names, before):
                pe.wait_ge(weights_split, n + 1)
                for i, name in enumerate(names):
                    pe.wait_ge(proj_taken, done(before[i]))
                    projection(SLOT[name], w, i, proj_ready)

            pair(w_a, N_CH, ("ch0", "ch1"), ("pool0", "pool1"))
            pair(w_b, N_CB, ("cb0", "cb1"), ("cc0", "cc1"))
            pe.wait_ge(wp_split, 1)
            for c in range(2):
                pe.wait_ge(pooled_split, c + 1)
                pe.wait_ge(proj_taken, done("ch%d" % c))
                for half in range(2):
                    for a, b in PASSES:
                        last = pe.matmul(ps[:, 2 * SLOT["pm%d" % c] + half, :], wp_r[:, a, c, :],
                                         hid0[:, b, c, half * BANK:(half + 1) * BANK],
                                         start=(a, b) == PASSES[0], stop=(a, b) == PASSES[-1])
                last.then_inc(proj_ready, 1)

            def outputs(n, first_slot, x0, before):
                pe.wait_ge(weights_split, n + 1)
                for k in range(KD):
                    if k < 4:
                        pe.wait_ge(proj_taken, done(before[k]))
                    else:
                        pe.wait_ge(x_updated, x0 + k - 3)
                    for half in range(2):
                        last = output(2 * ((first_slot + k) % 4) + half, w_o, hid0, k, half)
                    last.then_inc(x_psum_ready, 1)

            pe.wait_ge(proj_taken, done("pm1"))
            outputs(N_OUT_POOL, 2, X_MIX, ("cb0", "cb1", "pm0", "pm1"))
            for n, name in enumerate(("v0a", "v0b", "v1a", "v1b")):
                w = (w_a, w_b)[n // 2]
                pe.wait_ge(weights_split, (N_V0, N_V1)[n // 2] + 1)
                pe.wait_ge(x_updated, X_MIX + KD - 3 + n)
                for i in range(4):
                    c = 4 * (n % 2) + i
                    for k in range(KD):
                        for a, b in PASSES:
                            last = pe.matmul(unit(SLOT[name])[:, i * PAIR:(i + 1) * PAIR],
                                             xg[:, b, k, c * P:(c + 1) * P], w[:, a, k, :],
                                             start=(k == 0 and (a, b) == PASSES[0]),
                                             stop=(k == KD - 1 and (a, b) == PASSES[-1]))
                last.then_inc(proj_ready, 1)
            pe.wait_ge(wf_split, 1)
            pe.wait_ge(proj_taken, done("v0a"))
            for half in range(2):
                for k in range(KD):
                    for b in (LO, HI):
                        last = pe.matmul(ps[:, 2 * SLOT["f"] + half, :], wf[:, k, :],
                                         xg[:, b, k, half * BANK:(half + 1) * BANK],
                                         start=(k == 0 and b == LO), stop=(k == KD - 1 and b == HI))
            last.then_inc(proj_ready, 1)
            pe.wait_ge(conv_y_split, 2)
            outputs(N_OUT_CONV, 3, X_MIX + KD, ("v0b", "v1a", "v1b", "f"))
            for n, (w, pairs, names) in enumerate((
                    (w_b, N_Q0, ("q0", "q1")), (w_a, N_Q1, ("q2", "q3")),
                    (w_b, N_K0, ("k0", "k1")), (w_a, N_K1, ("k2", "k3")))):
                pe.wait_ge(weights_split, pairs + 1)
                for i, name in enumerate(names):
                    if n < 2:
                        pe.wait_ge(x_updated, X_MIX + 2 * KD - 3 + 2 * n + i)
                    else:
                        pe.wait_ge(proj_taken, done("q%d" % (2 * (n - 2) + i)))
                    projection(SLOT[name], w, i, proj_ready)

            pe.wait_ge(proj_taken, done("k3"))
            pe.wait_ge(consts_rounded, 1)

            def attention_output(k, chunks):
                for half in range(2):
                    cols = slice(half * BANK, (half + 1) * BANK)
                    for q in chunks:
                        for a, b in PASSES:
                            last = pe.matmul(ps[:, 2 * (k % 4) + half, :],
                                             out_w[q // 2][:, a, q % 2, k * P:(k + 1) * P],
                                             (y_hi, y_lo)[b][:, q, cols],
                                             start=(q == 0 and (a, b) == PASSES[0]),
                                             stop=(q == 3 and (a, b) == PASSES[-1]))
                return last

            def iteration(t, j):
                if t >= 5 and t % 2 == 1 and (t - 5) // 2 < STEPS // 2:
                    g = (t - 5) // 2
                    b, q = g // HEAD_GROUPS % 2, g % HEAD_GROUPS
                    if q == 0:
                        pe.wait_ge(value_split, heads_done(g // HEAD_GROUPS, j))
                    pe.wait_ge(pt_split, banks_done(2 * g + 1, j))
                    if g >= 2:
                        pe.wait_ge(y_summed, groups_done(g - 2, j))
                    chunks = 2 * q + 2
                    for c in range(chunks):
                        start = max(0, c * P - q * QG)
                        for part in (LO, HI):
                            last = pe.matmul(ps[:, 6 + g % 2, start:QG], v_st[:, b, c, :],
                                             pt[:, part, c, start:QG],
                                             start=(c == 0 and part == LO),
                                             stop=(c == chunks - 1 and part == HI))
                    last.then_inc(pv_ready, 1)
                if LAG <= t < STEPS + LAG:
                    r = t - LAG
                    pe.wait_ge(prob_ready, steps_done(r, j))
                    for bank, part in pt_banks(r):
                        if r >= 1:
                            pe.wait_ge(pt_split, banks_done(r - 1, j, bank))
                        for c in range(part.start, part.stop):
                            last = pe.transpose(unit(2)[:, c * P:(c + 1) * P],
                                                prob[:, r % PROBS, c * P:(c + 1) * P], ident[:, :])
                    last.then_inc(transposed, 1)
                if t < STEPS:
                    h, qb, s = t // NT, t % NT, t % 2
                    b, n = h % 2, P * (qb + 1)
                    if qb == 0:
                        pe.wait_ge(decay_picked, heads_done(h, j))
                        pe.wait_ge(query_split, heads_done(h, j))
                        pe.wait_ge(key_stacked, heads_done(h, j))
                    if t >= 2:
                        pe.wait_ge(exp_done, steps_done(t - 2, j))
                    queries = slice(qb * P, (qb + 1) * P)
                    for bank in range((n + BANK - 1) // BANK):
                        keys = slice(bank * BANK, min(n, (bank + 1) * BANK))
                        diagonal = keys.stop == n
                        dst = unit(s)[:, keys]
                        pe.matmul(dst, q_st[:, b, queries], k_lo[:, b, keys],
                                  start=True, stop=False)
                        pe.matmul(dst, q_st[:, b, queries], k_hi[:, b, keys],
                                  start=False, stop=False)
                        pe.matmul(dst, decay_q[:, queries], decay_h[:, b, keys],
                                  start=False, stop=not diagonal)
                    pe.matmul(unit(s)[:, queries], ident_r[:, :], causal_r[:, :],
                              start=False, stop=True).then_inc(scores_ready, 1)
                if t == STEPS + LAG - 1:
                    pe.wait_ge(weights_split, N_OUT_A1 + 1)
                    pe.wait_ge(attn_y_split, 6)
                    pe.wait_ge(exp_done, STEPS)
                    attention_output(0, range(3))
                if t == STEPS + LAG:
                    attention_output(1, range(3))
                    attention_output(2, range(3))

            pipeline(pe, iteration)
            pe.wait_ge(attn_y_split, 8)
            for k in range(KD):
                if k == 3:
                    pe.wait_ge(y_summed, STEPS // 2)
                if k >= 4:
                    pe.wait_ge(x_updated, X_ATTN + k - 3)
                attention_output(k, range(3, 4) if k < 3 else range(4)).then_inc(x_psum_ready, 1)

            swiglu(1)

            sum_rows(3)
            for c in range(NT):
                if c == 3:
                    pe.wait_ge(r_col_ready, 4)
                if c >= 4:
                    pe.wait_ge(out_ready[c % 2], c // 2 - 1)
                pe.wait_ge(gained, KD)
                for k in range(KD):
                    last = pe.transpose(unit(c % 4)[:, k * P:(k + 1) * P],
                                        x_gain[:, k, c * P:(c + 1) * P], ident[:, :])
                last.then_inc(out_psum_ready, 1)


def kernel(**inputs):
    import numpy as np
    import concourse.bacc as bacc
    from concourse.bass_utils import run_bass_kernel_spmd

    def chunked(a):
        return np.ascontiguousarray(np.asarray(a).reshape(-1, P).T)

    inv_counts = np.zeros((P, 2, WMAX), np.float32)
    for g, w in enumerate(WINDOWS):
        rows = slice((g % 2) * HD, (g % 2 + 1) * HD)
        inv_counts[rows, g // 2, :] = 1.0 / np.minimum(np.arange(WMAX) + 1, w)
    forget = np.zeros((P, 1), np.float32)
    forget[:HEADS, 0] = np.asarray(inputs["b_forget"])[0]
    taps = np.asarray(inputs["conv_w"])[0].reshape(TAPS, 2, P).transpose(2, 1, 0)
    vectors = np.concatenate(
        [chunked(inputs[n]) for n in ("norm_ffn1", "norm_mix", "norm_ffn2", "norm_final")]
        + [taps.reshape(P, 2 * TAPS), chunked(inputs["pool_scale"]), forget,
           inv_counts.reshape(P, 2 * WMAX)], axis=1)
    arrays = {
        "x": np.asarray(inputs["x"])[0],
        "w1_in": np.asarray(inputs["w_ffn1_in"])[0], "w1_out": np.asarray(inputs["w_ffn1_out"])[0],
        "wm_in": np.asarray(inputs["w_mix_in"])[0], "wm_out": np.asarray(inputs["w_mix_out"])[0],
        "w_pool": np.asarray(inputs["w_pool"])[0],
        "w2_in": np.asarray(inputs["w_ffn2_in"])[0], "w2_out": np.asarray(inputs["w_ffn2_out"])[0],
        "vectors": vectors,
    }
    nc = bacc.Bacc("TRN2", target_bir_lowering=False, num_devices=1)
    arrays = {"in_" + n: np.ascontiguousarray(a) for n, a in arrays.items()}
    args = [nc.dram_tensor(n, a.shape, mybir.dt.from_np(a.dtype), kind="ExternalInput").ap()
            for n, a in arrays.items()]
    out = nc.dram_tensor("out_x", (T, D), F32, kind="ExternalOutput").ap()
    trunk(nc, *args, out)
    result = run_bass_kernel_spmd(nc, [arrays], core_ids=[0])
    return result.results[0]["out_x"].reshape(1, T, D)
```

```python
from contextlib import ExitStack

import concourse.bass as bass
from concourse import mybir

F32 = mybir.dt.float32
F32R = mybir.dt.float32r
ALU = mybir.AluOpType
ACT = mybir.ActivationFunctionType
AX = mybir.AxisListType

P = 128
D = 1024
T = 1024
KD = D // P
NT = T // P
BANK = 512
F = 2816
PAIR = 2 * P
GROUPS = F // PAIR
TURNS = (GROUPS - 1) // 2
HEADS = 8
HD = 64
D_ATTN = HEADS * HD
COL_Q, COL_K, COL_V = 0, D_ATTN, 2 * D_ATTN
COL_F = 3 * D_ATTN
COL_POOL = COL_F + HEADS
COL_CB = COL_POOL + PAIR
COL_CC = COL_CB + PAIR
COL_CH = COL_CC + PAIR
WINDOWS = (2, 4, 8, 16)
WMAX = WINDOWS[-1]
TAPS = 3
EPS = 1e-6
SCALE = HD ** -0.5
MASKED = -1.0e30
HI, LO = 0, 1
PASSES = ((LO, HI), (HI, LO), (HI, HI))

V_NORM1, V_MIX, V_NORM2, V_FINAL = 0, KD, 2 * KD, 3 * KD
V_CONV = 4 * KD
V_PSCALE = V_CONV + 2 * TAPS
V_BFORGET = V_PSCALE + 2
V_COUNT = V_BFORGET + 1
V_ALL = V_COUNT + 2 * WMAX

(N_POOL, N_CC, N_CH, N_CB, N_OUT_POOL, N_V0, N_V1, N_OUT_CONV,
 N_Q0, N_Q1, N_K0, N_K1, N_OUT_A0, N_OUT_A1) = range(3 * GROUPS, 3 * GROUPS + 14)
N_FFN = (0, N_OUT_A1 + 1)

X_FFN1 = 2 * KD
X_MIX = X_FFN1 + KD * GROUPS
X_ATTN = X_MIX + 2 * KD
X_FFN2 = X_ATTN + KD
X_END = X_FFN2 + KD * GROUPS
X_BASE = (X_FFN1, X_FFN2)

LAG = 2
QG = 2 * P
STEPS = HEADS * NT
TURN = 2 * NT
HEAD_GROUPS = T // QG
TURN_GROUPS = 2 * HEAD_GROUPS
FILL = 11
LOOPS = STEPS // TURN - 1
ITERATIONS = STEPS + 6
Y_HI_AT, Y_LO_AT = (0, 4), (1, 5)

KB = 1024
SBUF_START, SBUF_END = 16512, 229344


def gate_pair(g):
    return 3 * g - 1 if g else 0


def down_pair(g):
    return 3 * g + 4 if g < GROUPS - 1 else 3 * GROUPS - 1


def trunk(nc, x, w1_in, w1_out, wm_in, wm_out, w_pool, w2_in, w2_out, vectors, out):
    with ExitStack() as ctx:
        def sem(name):
            return ctx.enter_context(nc.semaphore(name))

        place = [SBUF_START]

        def at(offset, name, shape, dt):
            size = 4
            for n in shape[1:]:
                size *= n
            assert offset + size <= SBUF_END, (name, offset + size - SBUF_END)
            return nc.alloc_sbuf_tensor_at(name, shape, dt, offset=offset)

        def keep(name, shape, dt):
            size = 4
            for n in shape[1:]:
                size *= n
            offset = place[0]
            place[0] += (size + 31) // 32 * 32
            return at(offset, name, shape, dt)

        xt = keep("xt", [P, KD, T], F32)
        r_rows = keep("r_rows", [P, T], F32)
        raw = keep("raw", [P, 2, KD * PAIR], F32)
        vec = keep("vec", [P, V_ALL], F32)
        ident = keep("ident", [P, P], F32)
        ident_r = keep("ident_r", [P, P], F32R)
        causal_r = keep("causal_r", [P, P], F32R)
        tri = keep("tri", [P, P], F32)
        ones2 = keep("ones2", [P, 2], F32)
        head_mask = keep("head_mask", [P, HEADS], F32)
        ms = keep("ms", [P, NT], F32)
        root = keep("root", [P, NT], F32)
        newton = keep("newton", [P, NT], F32)
        r_col = keep("r_col", [P, NT], F32)
        sums_x = keep("sums_x", [P, NT], F32)
        minus_max = keep("minus_max", [P, 2], F32)
        exp_sum = keep("exp_sum", [P, 2], F32)
        exp_inv = keep("exp_inv", [P, NT], F32)
        head_col = keep("head_col", [P, 1], F32)
        wf_raw = keep("wf_raw", [P, KD, HEADS], F32)

        a0 = place[0]
        xg = at(a0, "xg", [P, 2, KD, T], F32R)
        w_a = at(a0 + 64 * KB, "w_a", [P, 2, KD, PAIR], F32R)
        w_b = at(a0 + 80 * KB, "w_b", [P, 2, KD, PAIR], F32R)
        w_o = at(a0 + 96 * KB, "w_o", [P, 2, 2, D], F32R)
        w_b_rows = at(a0 + 80 * KB, "w_b_rows", [P, 2, 2, D], F32R)
        w_c = at(a0 + 96 * KB, "w_c", [P, 2, KD, PAIR], F32R)
        hid0 = at(a0 + 112 * KB, "hid0", [P, 2, 2, T], F32R)
        hid1 = at(a0 + 128 * KB, "hid1", [P, 2, 2, T], F32R)
        tmp = at(a0 + 144 * KB, "tmp", [P, 2, T], F32)
        hid = (hid0, hid1)
        x_in = at(a0 + 96 * KB, "x_in", [P, NT, D], F32)
        x_squares = at(a0 + 128 * KB, "x_squares", [P, 4, D], F32)
        mix = at(a0 + 128 * KB, "mix", [P, 3 * T + 32], F32)
        wp_raw = at(a0 + 141 * KB, "wp_raw", [P, 2, P], F32)
        wp_r = at(a0 + 142 * KB, "wp_r", [P, 2, 2, P], F32R)
        v_plain = at(a0 + 128 * KB, "v_plain", [P, NT, D_ATTN], F32)
        q_plain = at(a0 + 96 * KB, "q_plain", [P, 4, T], F32)
        k_plain = at(a0 + 112 * KB, "k_plain", [P, 4, T], F32)
        q_st = at(a0 + 0 * KB, "q_st", [P, 2, T], F32R)
        k_hi = at(a0 + 8 * KB, "k_hi", [P, 2, T], F32R)
        k_lo = at(a0 + 16 * KB, "k_lo", [P, 2, T], F32R)
        v_st = at(a0 + 24 * KB, "v_st", [P, 2, NT, 2 * HD], F32R)
        decay_k = at(a0 + 64 * KB, "decay_k", [P, T], F32R)
        decay_h = at(a0 + 68 * KB, "decay_h", [P, 2, T], F32R)
        decay_q = at(a0 + 76 * KB, "decay_q", [P, T], F32R)
        pt = (at(a0 + 48 * KB, "pt0", [P, 2, NT, QG], F32R),
              at(a0 + 32 * KB, "pt1", [P, 2, NT, QG], F32R))
        out_w = (w_b_rows,
                 at(a0 + 128 * KB, "out_w1", [P, 2, 2, D], F32R))
        y_hi = at(a0 + 96 * KB, "y_hi", [P, 4, T], F32R)
        y_lo = at(a0 + 112 * KB, "y_lo", [P, 4, T], F32R)
        y_f = tmp[:, 0, :]
        prob = (r_rows[:, :], tmp[:, 1, :])
        x_gain = at(a0, "x_gain", [P, KD, T], F32)
        x_out = at(a0 + 32 * KB, "x_out", [P, NT, D], F32)

        wf = w_b[:, HI, :, 0:P]

        def row(s, quadrant):
            return tmp[32 * quadrant:32 * quadrant + HEADS, s, :]

        pool_u = mix[:, 0:T]
        pool_a = mix[:, T:2 * T + WMAX]
        pool_b = mix[:, 2 * T + WMAX:3 * T + 2 * WMAX]
        conv_cc = tmp
        conv_u = mix[:, 0:2 * (T + 2)].rearrange("p (c t) -> p c t", c=2)
        conv_b = mix[:, 2 * T + 16:3 * T + 16]

        ps = ctx.enter_context(nc.psum_tensor("ps", [P, 8, BANK], F32))

        def unit(slot):
            return ps[:, 2 * slot:2 * slot + 2, :].rearrange("p b n -> p (b n)")

        def f32(ap):
            return ap.bitcast(F32)

        def halves(b):
            return slice(HD * b, HD * b + HD), slice(HD - HD * b, P - HD * b)

        def of_pair(a, rows, h, j):
            return a[rows, bass.ds(h // 2 + j, 1), :].rearrange("p a t -> p (a t)")

        def v_of(h, j):
            return v_plain[:, :, bass.ds(HD * h + 2 * HD * j, HD)]

        def y_of(g):
            rows, _ = halves(g // HEAD_GROUPS % 2)
            q = g % HEAD_GROUPS
            return y_f[rows, q * QG:(q + 1) * QG]

        def pipeline(engine, iteration):
            for t in range(FILL):
                iteration(t, 0)
            with engine.Fori(0, LOOPS) as j:
                for t in range(FILL, FILL + TURN):
                    iteration(t, j)
            for t in range(FILL + LOOPS * TURN, ITERATIONS):
                iteration(t, 0)

        def blocks(t, offset):
            h, rest = divmod(t - offset, NT)
            return h + 1 if rest == 0 and 0 <= h + 1 < HEADS else None

        def banks_done(r, j, bank=1):
            count = [min(i, 4) + 2 * max(i - 4, 0) for i in range(NT + 1)]
            return (r // NT * count[NT] + (count[r % NT] + 1 if bank == 0 else count[r % NT + 1])
                    + 2 * count[NT] * j)

        def pt_banks(r):
            nk = r % NT + 1
            return [(0, slice(0, min(nk, 4)))] + ([(1, slice(4, nk))] if nk > 4 else [])

        def chunks_in_psum(keys):
            return unit(2)[:, keys.start * P:keys.stop * P]\
                .rearrange("p (k q) -> p k q", k=keys.stop - keys.start)

        def steps_done(r, j):
            return r + 1 + TURN * j

        def groups_done(g, j):
            return g + 1 + TURN_GROUPS * j

        def heads_done(h, j):
            return h + 1 + 2 * j

        def flat(w, part):
            return w[:, part, :, :].rearrange("p a b -> p (a b)")

        x_loaded = [sem("x_loaded%d" % c) for c in range(4)]
        vec_loaded = sem("vec_loaded")
        wf_loaded = sem("wf_loaded")
        wp_loaded = sem("wp_loaded")
        raw_loaded = (sem("raw_loaded_even"), sem("raw_loaded_odd"))
        out_stored = sem("out_stored")
        consts_ready = sem("consts_ready")
        consts_cleared = sem("consts_cleared")
        wp_cleared = sem("wp_cleared")
        consts_rounded = sem("consts_rounded")
        mask_ready = sem("mask_ready")
        weights_hi = sem("weights_hi")
        weights_split = sem("weights_split")
        wp_hi = sem("wp_hi")
        wp_split = sem("wp_split")
        wf_hi = sem("wf_hi")
        wf_split = sem("wf_split")
        x_psum_ready = sem("x_psum_ready")
        x_updated = sem("x_updated")
        xg_hi = sem("xg_hi")
        xg_split = sem("xg_split")
        square_ready = sem("square_ready")
        input_squared = sem("input_squared")
        sumsq_added = sem("sumsq_added")
        r_sum_ready = sem("r_sum_ready")
        ms_ready = sem("ms_ready")
        root_ready = sem("root_ready")
        r_col_ready = sem("r_col_ready")
        r_bcast_ready = sem("r_bcast_ready")
        r_rows_ready = sem("r_rows_ready")
        gate_ready = sem("gate_ready")
        up_ready = sem("up_ready")
        gate_scaled = sem("gate_scaled")
        sigmoid_ready = sem("sigmoid_ready")
        gated = sem("gated")
        up_scaled = sem("up_scaled")
        hidden_ready = sem("hidden_ready")
        hidden_hi = sem("hidden_hi")
        hidden_split = sem("hidden_split")
        proj_ready = sem("proj_ready")
        proj_taken = sem("proj_taken")
        pooled_ready = sem("pooled_ready")
        pooled_hi = sem("pooled_hi")
        pooled_split = sem("pooled_split")
        pool_y_hi = sem("pool_y_hi")
        conv_y_ready = sem("conv_y_ready")
        conv_y_hi = sem("conv_y_hi")
        conv_y_split = sem("conv_y_split")
        chain = sem("vector_chain")
        forget_low = sem("forget_low")
        forget_abs = sem("forget_abs")
        forget_exp = sem("forget_exp")
        forget_sum = sem("forget_sum")
        forget_log = sem("forget_log")
        forget_lost = sem("forget_lost")
        forget_inv = sem("forget_inv")
        decay_summed = sem("decay_summed")
        decay_filled = sem("decay_filled")
        decay_hi = sem("decay_hi")
        decay_lo = sem("decay_lo")
        decay_ready = sem("decay_ready")
        xg_half_used = sem("xg_half_used")
        key_hi = sem("key_hi")
        query_hi = sem("query_hi")
        value_hi = sem("value_hi")
        key_lo = sem("key_lo")
        query_split = sem("query_split")
        value_split = sem("value_split")
        key_doubled = sem("key_doubled")
        key_stacked = sem("key_stacked")
        head_picked = sem("head_picked")
        decay_picked = sem("decay_picked")
        scores_ready = sem("scores_ready")
        max_ready = sem("max_ready")
        exp_done = sem("exp_done")
        inverted = sem("inverted")
        transposed = sem("transposed")
        pt_hi = sem("pt_hi")
        pt_split = sem("pt_split")
        pv_ready = sem("pv_ready")
        y_low = sem("y_low")
        y_added = sem("y_added")
        y_summed = sem("y_summed")
        attn_y_hi = sem("attn_y_hi")
        attn_y_split = sem("attn_y_split")
        gained = sem("gained")
        out_psum_ready = sem("out_psum_ready")
        out_ready = (sem("out_ready_vector"), sem("out_ready_scalar"))

        UNITS = ("pool0", "pool1", "cc0", "cc1", "ch0", "ch1", "cb0", "cb1", "pm0", "pm1",
                 "v0a", "v0b", "v1a", "v1b", "f", "q0", "q1", "q2", "q3", "k0", "k1", "k2", "k3")
        SLOT = dict(zip(UNITS, (0, 1, 2, 3, 0, 1, 2, 3, 0, 1,
                                2, 3, 0, 1, 2, 3, 0, 1, 2, 3, 0, 1, 2)))
        NORM_SLOT = 3

        def done(name):
            return UNITS.index(name) + 1

        def counter(c, j):
            return lambda m, a: m * c + a + 2 * m * j

        def pair_at(base, n, j):
            return (base + n) % 2, 16 * ((base + n) // 2 + 1) + 48 * j

        block = ctx.enter_context(nc.Block())

        @block.sync
        def _(sp):
            def columns(w, col):
                return w.rearrange("(k p) f -> p k f", p=P)[:, :, bass.ds(col, PAIR)]

            def rows(w, chunk):
                return w.rearrange("(c p) d -> p c d", p=P)[:, bass.ds(chunk, 2), :]

            def load(base, n, j, src, chunks):
                slot, _ = pair_at(base, n, j)
                if base + n >= 2:
                    sp.wait_ge(weights_split, base + n - 1 + 6 * j)
                dst = raw[:, slot, :].rearrange("p (c f) -> p c f", c=chunks)
                sp.dma_start(dst, src).then_inc(raw_loaded[slot], 16)

            def load_x(half):
                for c in (2 * half, 2 * half + 1):
                    sp.dma_start(x_in[:, 2 * c:2 * c + 2, :],
                                 x.rearrange("(c p) d -> p c d", p=P)[:, 2 * c:2 * c + 2, :])\
                        .then_inc(x_loaded[c], 16)

            def swiglu(s, w_in, w_out):
                def gate_up(c, j):
                    group = counter(c, j)
                    load(N_FFN[s], gate_pair(c), j, columns(w_in, group(PAIR, 0)), KD)
                    load(N_FFN[s], gate_pair(c) + 1, j, columns(w_in, group(PAIR, F)), KD)

                def down(c, j):
                    load(N_FFN[s], down_pair(c), j, rows(w_out, counter(c, j)(2, 0)), 2)

                if s == 0:
                    load_x(0)
                    load(0, 0, 0, columns(w_in, 0), KD)
                    load_x(1)
                    load(0, 1, 0, columns(w_in, F), KD)
                else:
                    gate_up(0, 0)
                gate_up(1, 0)
                down(0, 0)
                with sp.Fori(0, TURNS - 1) as j:
                    for c in (1, 2):
                        gate_up(c + 1, j)
                        down(c, j)
                gate_up(GROUPS - 1, 0)
                down(GROUPS - 2, 0)
                down(GROUPS - 1, 0)

            swiglu(0, w1_in, w1_out)
            for n, src, chunks in (
                    (N_POOL, columns(wm_in, COL_POOL), KD), (N_CC, columns(wm_in, COL_CC), KD),
                    (N_CH, columns(wm_in, COL_CH), KD), (N_CB, columns(wm_in, COL_CB), KD),
                    (N_OUT_POOL, rows(wm_out, 4), 2),
                    (N_V0, columns(wm_in, COL_V), KD), (N_V1, columns(wm_in, COL_V + PAIR), KD),
                    (N_OUT_CONV, rows(wm_out, 6), 2),
                    (N_Q0, columns(wm_in, COL_Q), KD), (N_Q1, columns(wm_in, COL_Q + PAIR), KD),
                    (N_K0, columns(wm_in, COL_K), KD), (N_K1, columns(wm_in, COL_K + PAIR), KD),
                    (N_OUT_A0, rows(wm_out, 0), 2), (N_OUT_A1, rows(wm_out, 2), 2)):
                load(0, n, 0, src, chunks)
            swiglu(1, w2_in, w2_out)
            for c in range(NT):
                sp.wait_ge(out_ready[c % 2], c // 2 + 1)
                sp.dma_start(out[c * P:(c + 1) * P, :], x_out[:, c, :]).then_inc(out_stored, 16)
            sp.wait_ge(out_stored, 16 * NT)

        @block.gpsimd
        def _(pool):
            pool.dma_start(vec[:, :], vectors).then_inc(vec_loaded, 16)
            pool.dma_start(wf_raw[:, :, :], wm_in.rearrange("(k p) f -> p k f", p=P)
                           [:, :, COL_F:COL_F + HEADS]).then_inc(wf_loaded, 16)
            pool.memset(ones2[:, :], 1.0)
            pool.memset(tri[:, :], 0.0)
            pool.memset(ident[:, :], 0.0).then_inc(consts_cleared, 1)
            pool.wait_ge(consts_cleared, 1)
            pool.affine_select(out=ident[:, :], in_=ident[:, :], compare_op=ALU.not_equal, fill=1.0,
                               base=0, pattern=[[-1, P]], channel_multiplier=1)
            pool.affine_select(out=tri[:, :], in_=tri[:, :], compare_op=ALU.is_ge, fill=MASKED,
                               base=0, pattern=[[-1, P]], channel_multiplier=1)\
                .then_inc(consts_ready, 1)
            pool.wait_ge(r_rows_ready, 2)
            pool.memset(wp_raw[:, :, :], 0.0).then_inc(wp_cleared, 1)
            pool.wait_ge(wp_cleared, 1)
            for g in range(len(WINDOWS)):
                h = (g % 2) * HD
                pool.dma_start(wp_raw[h:h + HD, g // 2, h:h + HD], w_pool[g, :, :])\
                    .then_inc(wp_loaded, 16)

            for h in range(1, HEADS):
                b = h % 2
                own, other = halves(b)
                pool.wait_ge(key_stacked, h)
                pool.tensor_copy(head_col[:, :], head_mask[:, h:h + 1]).then_inc(head_picked, 1)
                pool.wait_ge(head_picked, h)
                if h >= 2:
                    pool.wait_ge(scores_ready, NT * (h - 1))
                pool.tensor_scalar(decay_h[:, b, :], f32(decay_k[:, :]), head_col[:, 0:1], None,
                                   ALU.mult).then_inc(decay_picked, 1)
                pool.wait_ge(decay_picked, h + 1)
                pool.wait_ge(key_hi, h + 1)
                pool.tensor_copy(k_hi[other, b, :], f32(k_hi[own, b, :])).then_inc(key_doubled, 1)
                pool.wait_ge(key_doubled, h + 1)
                pool.wait_ge(key_lo, h + 1)
                pool.tensor_copy(k_lo[other, b, :], f32(k_lo[own, b, :])).then_inc(key_stacked, 1)

        @block.scalar
        def _(act):
            def copy(dst, src, scale=1.0):
                return act.activation(dst, src, ACT.Copy, scale=scale)

            def split_hi(w, base, n, j=0):
                slot, loaded = pair_at(base, n, j)
                act.wait_ge(raw_loaded[slot], loaded)
                copy(flat(w, HI), raw[:, slot, :]).then_inc(weights_hi, 1)

            def gain_hi(k, v, cols=slice(0, T)):
                act.activation(xg[:, HI, k, cols], xt[:, k, cols], ACT.Identity,
                               scale=vec[:, v + k:v + k + 1]).then_inc(xg_hi, 1)

            def square(s, k):
                if k >= 2:
                    act.wait_ge(sumsq_added, (KD - 1) * (s - 1) + k - 1)
                act.activation(tmp[:, min(k, 1), :], xt[:, k, :], ACT.Square)\
                    .then_inc(square_ready, 1)

            def gain_all(s, before, v):
                for k in range(KD):
                    act.wait_ge(x_updated, before + k + 1)
                    gain_hi(k, v)
                    if k < KD // 2:
                        square(s, k)

            def other_squares(s):
                for k in range(KD // 2, KD):
                    square(s, k)

            def root_step(s):
                act.wait_ge(ms_ready, s + 1)
                act.activation(root[:, :], ms[:, :], ACT.Sqrt).then_inc(root_ready, 1)

            def swiglu(s):
                base, g0, x0 = N_FFN[s], 2 * GROUPS * s, X_BASE[s]

                def hidden(c, j, chunks=range(2)):
                    i = counter(c, j)
                    for f in chunks:
                        act.wait_ge(gate_scaled, i(2, g0 + f + 1))
                        act.activation(tmp[:, 1, :], tmp[:, 0, :], ACT.Sigmoid)\
                            .then_inc(sigmoid_ready, 1)
                        if f == 0 and c > 0:
                            act.wait_ge(x_psum_ready, i(KD, x0 - KD))
                        act.wait_ge(hidden_ready, i(2, g0 + f + 1))
                        copy(hid[c % 2][:, HI, f, :], tmp[:, 0, :]).then_inc(hidden_hi, 1)

                def split_gate(c, j):
                    act.wait_ge(gate_ready, counter(c, j)(2, g0))
                    split_hi(w_a, base, gate_pair(c), j)

                def split_up(c, j):
                    act.wait_ge(up_ready, counter(c, j)(2, g0))
                    split_hi(w_b, base, gate_pair(c) + 1, j)

                def split_down(c, j):
                    act.wait_ge(x_psum_ready, counter(c, j)(KD, x0))
                    split_hi(w_o, base, down_pair(c), j)

                split_gate(1, 0)
                hidden(0, 0, (0,))
                split_up(1, 0)
                hidden(0, 0, (1,))
                split_down(0, 0)
                with act.Fori(0, TURNS - 1) as j:
                    for c in (1, 2):
                        hidden(c, j)
                        split_gate(c + 1, j)
                        split_up(c + 1, j)
                        split_down(c, j)
                hidden(GROUPS - 2, 0)
                split_gate(GROUPS - 1, 0)
                split_up(GROUPS - 1, 0)
                split_down(GROUPS - 2, 0)
                hidden(GROUPS - 1, 0)
                act.wait_ge(up_ready, g0 + 2 * GROUPS)
                split_hi(w_b_rows, base, down_pair(GROUPS - 1))

            act.wait_ge(consts_ready, 1)
            copy(ident_r[:, :], ident[:, :])
            copy(causal_r[:, :], tri[:, :]).then_inc(consts_rounded, 1)
            act.wait_ge(vec_loaded, 16)
            for half in range(2):
                for k in range(KD):
                    act.wait_ge(x_updated, KD * half + k + 1)
                    gain_hi(k, V_NORM1, slice(BANK * half, BANK * (half + 1)))
                    if k % 2 == 1:
                        c = 4 * half + k // 2
                        act.wait_ge(x_loaded[c // 2], 16)
                        if c >= 4:
                            act.wait_ge(input_squared, c - 3)
                        act.activation(x_squares[:, c % 4, :], x_in[:, c, :], ACT.Square,
                                       accum_out=sums_x[:, c:c + 1]).then_inc(input_squared, 1)
                    if half == 0 and k == 5:
                        split_hi(w_a, 0, 0)
                    if half == 1 and k == 3:
                        split_hi(w_b, 0, 1)
            root_step(0)
            swiglu(0)

            act.wait_ge(gate_ready, 2 * GROUPS)
            split_hi(w_a, 0, N_POOL)
            act.wait_ge(x_psum_ready, X_MIX - KD)
            split_hi(w_c, 0, N_CC)
            gain_all(1, X_MIX - KD, V_MIX)
            act.wait_ge(x_psum_ready, X_MIX)
            split_hi(w_b, 0, N_CH)
            other_squares(1)
            act.wait_ge(proj_ready, done("pool1"))
            split_hi(w_a, 0, N_CB)
            root_step(1)
            act.wait_ge(wp_loaded, 16 * len(WINDOWS))
            copy(wp_r[:, HI, :, :], wp_raw[:, :, :]).then_inc(wp_hi, 1)
            act.wait_ge(pooled_ready, 1)
            copy(hid0[:, HI, 0, :], pool_u).then_inc(pooled_hi, 1)
            act.wait_ge(proj_ready, done("cc1"))
            split_hi(w_o, 0, N_OUT_POOL)
            act.wait_ge(pooled_ready, 2)
            copy(hid0[:, HI, 1, :], pool_u).then_inc(pooled_hi, 1)
            act.wait_ge(proj_ready, done("ch1"))
            split_hi(w_b, 0, N_V0)
            act.wait_ge(proj_ready, done("cb1"))
            split_hi(w_a, 0, N_V1)
            for c in range(2):
                act.wait_ge(proj_ready, done("pm%d" % c))
                act.activation(hid0[:, HI, c, :], unit(SLOT["pm%d" % c]), ACT.Identity,
                               scale=vec[:, V_PSCALE + c:V_PSCALE + c + 1]).then_inc(pool_y_hi, 1)
            act.wait_ge(proj_ready, done("v0b"))
            act.wait_ge(wf_loaded, 16)
            copy(wf[:, :, 0:HEADS], wf_raw[:, :, :]).then_inc(wf_hi, 1)
            act.wait_ge(x_psum_ready, X_MIX + KD)
            act.wait_ge(conv_y_ready, 2)
            for c in range(2):
                copy(hid0[:, HI, c, :], conv_cc[:, c, :]).then_inc(conv_y_hi, 1)
            split_hi(w_o, 0, N_OUT_CONV)
            act.wait_ge(proj_ready, done("v1b"))
            split_hi(w_a, 0, N_Q0)
            act.wait_ge(proj_ready, done("f"))
            act.wait_ge(conv_y_split, 2)
            copy(row(0, 0), unit(SLOT["f"])[32:32 + HEADS, :]).then_inc(forget_low, 1)
            split_hi(w_b, 0, N_Q1)
            act.wait_ge(forget_abs, 1)
            act.activation(row(0, 1), row(0, 0), ACT.Exp, scale=-1.0).then_inc(forget_exp, 1)
            act.wait_ge(forget_sum, 1)
            act.activation(row(0, 2), row(1, 1), ACT.Ln).then_inc(forget_log, 1)
            act.wait_ge(forget_log, 1)
            act.wait_ge(forget_lost, 1)
            act.activation(row(0, 1), row(0, 2), ACT.Exp, scale=-1.0).then_inc(forget_inv, 1)
            act.wait_ge(proj_ready, done("q1"))
            split_hi(w_a, 0, N_K0)
            act.wait_ge(proj_ready, done("q3"))
            split_hi(w_b, 0, N_K1)

            act.wait_ge(decay_filled, 1)
            act.wait_ge(decay_summed, 1)
            copy(decay_k[0:HEADS, :], row(1, 0)).then_inc(decay_hi, 1)
            act.wait_ge(decay_hi, 1)
            copy(decay_q[64:64 + HEADS, :], f32(decay_k[0:HEADS, :]), -1.0)
            act.wait_ge(decay_lo, 1)
            copy(decay_q[96:96 + HEADS, :], f32(decay_k[32:32 + HEADS, :]), -1.0)\
                .then_inc(decay_ready, 1)
            act.wait_ge(xg_half_used, 1)
            act.wait_ge(proj_taken, done("k0"))

            def keys(h, j):
                own, _ = halves(h % 2)
                if h >= 2:
                    act.wait_ge(pv_ready, groups_done(HEAD_GROUPS * (h - 1) - 1, j))
                copy(k_hi[own, h % 2, :], of_pair(k_plain, own, h, j)).then_inc(key_hi, 1)

            def queries(h, j):
                own, _ = halves(h % 2)
                copy(q_st[own, h % 2, :], of_pair(q_plain, own, h, j), SCALE).then_inc(query_hi, 1)

            def values(h, j):
                copy(v_st[:, h % 2, :, 0:HD], v_of(h, j)).then_inc(value_hi, 1)

            def iteration(t, j):
                if LAG <= t < STEPS + LAG:
                    r = t - LAG
                    to = P * (r % 2)
                    if r % 2 == 0 and r >= 4:
                        act.wait_ge(pv_ready, groups_done(r // 2 - 2, j))
                    for bank, part in pt_banks(r):
                        act.wait_ge(transposed, banks_done(r, j, bank))
                        copy(pt[r // 2 % 2][:, HI, part, to:to + P],
                             chunks_in_psum(part)).then_inc(pt_hi, 1)
                if t >= 5 and t % 2 == 1 and (t - 5) // 2 < STEPS // 2:
                    g = (t - 5) // 2
                    act.wait_ge(pv_ready, groups_done(g, j))
                    if g > 0 and g % TURN_GROUPS in (0, HEAD_GROUPS // 2):
                        before = 2 * (g // TURN_GROUPS) - 1 + g % TURN_GROUPS // 2
                        if before > 0:
                            act.wait_ge(attn_y_split, before + 2 * j)
                    copy(y_of(g), ps[HD:2 * HD, 6 + g % 2, 0:QG]).then_inc(y_low, 1)
                if t < STEPS:
                    s, n = t % 2, P * (t % NT + 1)
                    if t >= 2:
                        act.wait_ge(transposed, banks_done(t - 2, j))
                    act.wait_ge(max_ready, steps_done(t, j))
                    act.activation(prob[t % 2][:, 0:n], unit(s)[:, 0:n], ACT.Exp,
                                   bias=minus_max[:, s:s + 1],
                                   accum_out=exp_sum[:, t % 2:t % 2 + 1])\
                        .then_inc(exp_done, 1)
                if t >= TURN and t % TURN in Y_HI_AT:
                    pair, half = t // TURN - 1, Y_HI_AT.index(t % TURN)
                    last = HEAD_GROUPS + HEAD_GROUPS // 2 * (half + 1) - 1
                    cols = slice(half * BANK, (half + 1) * BANK)
                    act.wait_ge(y_summed, groups_done(TURN_GROUPS * pair + last, j))
                    copy(y_hi[:, bass.ds(pair + j, 1), cols].rearrange("p a t -> p (a t)"),
                         y_f[:, cols]).then_inc(attn_y_hi, 1)
                for offset, stage in ((3, keys), (4, queries), (NT + 1, values)):
                    h = blocks(t, offset)
                    if h is not None:
                        stage(h, j)
                if t == STEPS - 5:
                    split_hi(out_w[0], 0, N_OUT_A0)
                if t == STEPS - 4:
                    act.wait_ge(value_split, HEADS)
                    split_hi(out_w[1], 0, N_OUT_A1)

            queries(0, 0)
            keys(0, 0)
            copy(k_hi[HD:, 0, :], k_plain[0:HD, 0, :]).then_inc(key_doubled, 1)
            act.wait_ge(proj_ready, done("k3"))
            pipeline(act, iteration)

            split_hi(w_a, N_FFN[1], 0)
            gain_all(2, X_FFN2 - KD, V_NORM2)
            act.wait_ge(x_psum_ready, X_FFN2)
            split_hi(w_b, N_FFN[1], 1)
            other_squares(2)
            root_step(2)
            swiglu(1)
            act.wait_ge(up_ready, 4 * GROUPS)
            for k in range(KD):
                act.wait_ge(x_updated, X_END - KD + k + 1)
                square(3, k)
                act.activation(x_gain[:, k, :], xt[:, k, :], ACT.Identity,
                               scale=vec[:, V_FINAL + k:V_FINAL + k + 1]).then_inc(gained, 1)
            root_step(3)
            act.wait_ge(r_col_ready, 4)
            for c in range(1, NT, 2):
                act.wait_ge(out_psum_ready, c + 1)
                act.activation(x_out[:, c, :], unit(c % 4), ACT.Identity,
                               scale=r_col[:, c:c + 1]).then_inc(out_ready[1], 1)

        @block.vector
        def _(dve):
            steps = [0]

            def link(ins):
                steps[0] += 1
                ins.then_inc(chain, 1)
                dve.wait_ge(chain, steps[0])

            def mul(dst, a, b):
                return dve.tensor_tensor(out=dst, in0=a, in1=b, op=ALU.mult)

            def add(dst, a, b):
                return dve.tensor_tensor(out=dst, in0=a, in1=b, op=ALU.add)

            def lo_part(dst, value, hi):
                return dve.tensor_tensor(out=dst, in0=value, in1=f32(hi), op=ALU.subtract)

            def scaled_lo(dst, value, scale, hi):
                return dve.scalar_tensor_tensor(out=dst, in0=value, scalar=scale, in1=f32(hi),
                                                op0=ALU.mult, op1=ALU.subtract)

            def split_lo(w, base, n, j=0):
                slot, _ = pair_at(base, n, j)
                dve.wait_ge(weights_hi, base + n + 1 + 6 * j)
                lo_part(flat(w, LO), raw[:, slot, :], flat(w, HI)).then_inc(weights_split, 1)

            def gain_lo(s, k, v, cols=slice(0, T)):
                dve.wait_ge(xg_hi, KD * (s + 1) + k + 1)
                scaled_lo(xg[:, LO, k, cols], xt[:, k, cols], vec[:, v + k:v + k + 1],
                          xg[:, HI, k, cols])\
                    .then_inc(xg_split, 1)

            def residual(k, factor, at_count, last_count, cols=slice(0, T), psum=None):
                dve.wait_ge(x_psum_ready, at_count)
                dve.wait_ge(x_updated, last_count)
                dve.scalar_tensor_tensor(out=xt[:, k, cols], in0=psum, scalar=factor,
                                         in1=xt[:, k, cols], op0=ALU.mult, op1=ALU.add)\
                    .then_inc(x_updated, 1)

            def sum_square(s, k):
                dve.wait_ge(square_ready, KD * (s - 1) + k + 1)
                if k >= 2:
                    dve.wait_ge(sumsq_added, (KD - 1) * (s - 1) + k - 1)
                add(tmp[:, 0, :], tmp[:, 0, :], tmp[:, 1, :]).then_inc(sumsq_added, 1)

            def inverse_rms(s):
                if s == 0:
                    dve.wait_ge(input_squared, NT)
                    sums = sums_x[:, :]
                else:
                    dve.wait_ge(r_sum_ready, s)
                    sums = ps[:, 2 * NORM_SLOT, 0:2 * NT]\
                        .rearrange("p (c two) -> p c two", two=2)[:, :, 0]
                dve.tensor_scalar(ms[:, :], sums, 1.0 / D, EPS, ALU.mult, ALU.add)\
                    .then_inc(ms_ready, 1)
                dve.wait_ge(root_ready, s + 1)
                link(dve.reciprocal(root[:, :], root[:, :]))
                link(mul(newton[:, :], root[:, :], root[:, :]))
                link(mul(newton[:, :], newton[:, :], ms[:, :]))
                link(dve.tensor_scalar(newton[:, :], newton[:, :], -0.5, 1.5, ALU.mult, ALU.add))
                mul(r_col[:, :], root[:, :], newton[:, :]).then_inc(r_col_ready, 1)

            def spread_rms(s):
                dve.wait_ge(r_bcast_ready, s + 1)
                dve.tensor_copy(r_rows[:, :], unit(NORM_SLOT)).then_inc(r_rows_ready, 1)
                dve.wait_ge(r_rows_ready, s + 1)

            def gain_all(s, v, update):
                for k in range(KD + 1):
                    if k < KD:
                        update(k)
                    if k > 0:
                        gain_lo(s, k - 1, v)
                    if 1 < k <= KD // 2:
                        sum_square(s, k - 1)

            def other_squares(s):
                for k in range(KD // 2, KD):
                    sum_square(s, k)

            def norm(s):
                inverse_rms(s)
                spread_rms(s)

            def swiglu(s, tail):
                base, g0, x0 = N_FFN[s], 2 * GROUPS * s, X_BASE[s]

                def hidden(c, j, chunks=range(2)):
                    i = counter(c, j)
                    for f in chunks:
                        now = i(2, g0 + f + 1)
                        dve.wait_ge(gate_ready, now)
                        if c > 0 or f > 0:
                            dve.wait_ge(hidden_split, now - 1)
                        mul(tmp[:, 0, :], unit(2 * f), r_rows[:, :]).then_inc(gate_scaled, 1)
                        dve.wait_ge(sigmoid_ready, now)
                        mul(tmp[:, 0, :], tmp[:, 0, :], tmp[:, 1, :]).then_inc(gated, 1)
                        dve.wait_ge(gated, now)
                        dve.wait_ge(up_ready, now)
                        mul(tmp[:, 1, :], unit(2 * f + 1), r_rows[:, :]).then_inc(up_scaled, 1)
                        dve.wait_ge(up_scaled, now)
                        mul(tmp[:, 0, :], tmp[:, 0, :], tmp[:, 1, :]).then_inc(hidden_ready, 1)
                        dve.wait_ge(hidden_hi, now)
                        lo_part(hid[c % 2][:, LO, f, :], tmp[:, 0, :], hid[c % 2][:, HI, f, :])\
                            .then_inc(hidden_split, 1)

                def update(c, j, k):
                    i = counter(c, j)
                    residual(k, 0.5, i(KD, x0 + k + 1), i(KD, x0 + k + 1 - KD), psum=unit(k % 4))

                def split_gate(c, j):
                    split_lo(w_a, base, gate_pair(c), j)

                def split_up(c, j):
                    split_lo(w_b, base, gate_pair(c) + 1, j)

                def split_down(c, j):
                    split_lo(w_o, base, down_pair(c), j)

                def step(c, j, more):
                    hidden(c, j)
                    if not more:
                        split_lo(w_b_rows, base, down_pair(c), j)
                    for k in range(KD):
                        update(c - 1, j, k)
                        if more and k == 1:
                            split_gate(c + 1, j)
                        if more and k == 3:
                            split_up(c + 1, j)
                    if more:
                        split_down(c, j)

                split_gate(1, 0)
                hidden(0, 0, (0,))
                split_up(1, 0)
                hidden(0, 0, (1,))
                split_down(0, 0)
                with dve.Fori(0, TURNS - 1) as j:
                    step(1, j, True)
                    step(2, j, True)
                step(GROUPS - 2, 0, True)
                step(GROUPS - 1, 0, False)
                tail(lambda k: update(GROUPS - 1, 0, k))

            dve.wait_ge(consts_ready, 1)
            dve.tensor_reduce(head_mask[:, :], ident[:, :].rearrange("p (q h) -> p h q", q=4)
                              [:, 0:HEADS, :], AX.X, ALU.add).then_inc(mask_ready, 1)
            dve.wait_ge(vec_loaded, 16)
            for half in range(2):
                cols = slice(BANK * half, BANK * (half + 1))
                for k in range(KD + 1):
                    if k < KD:
                        dve.wait_ge(x_psum_ready, KD * half + k + 1)
                        dve.tensor_copy(xt[:, k, cols], ps[:, k, :]).then_inc(x_updated, 1)
                    if k > 0:
                        dve.wait_ge(x_updated, KD * half + k)
                        gain_lo(half - 1, k - 1, V_NORM1, cols)
                split_lo((w_a, w_b)[half], 0, half)
            norm(0)

            def before_mixer(update):
                split_lo(w_a, 0, N_POOL)
                split_lo(w_c, 0, N_CC)
                gain_all(1, V_MIX, update)
                split_lo(w_b, 0, N_CH)
                other_squares(1)
                split_lo(w_a, 0, N_CB)
                norm(1)

            swiglu(0, before_mixer)

            def take(name, dst):
                dve.wait_ge(proj_ready, done(name))
                return mul(dst, unit(SLOT[name]), r_rows[:, :])

            def taken_and_linked(name, ins):
                ins.then_inc(proj_taken, 1)
                dve.wait_ge(proj_taken, done(name))

            def window(dst, src, shift, rows=slice(0, P)):
                link(add(dst[rows, WMAX:], src[rows, WMAX:],
                         src[rows, WMAX - shift:T + WMAX - shift]))

            upper = slice(HD, P)
            dve.memset(pool_a[:, 0:WMAX], 0.0)
            link(dve.memset(pool_b[:, 0:WMAX], 0.0))
            for c in range(2):
                if c > 0:
                    dve.wait_ge(pooled_split, c)
                taken_and_linked("pool%d" % c, take("pool%d" % c, pool_u))
                if c > 0:
                    for i in range(2):
                        take("cc%d" % i, conv_cc[:, i, :]).then_inc(proj_taken, 1)
                add(pool_a[:, WMAX + 1:], pool_u[:, 1:], pool_u[:, 0:T - 1])
                link(dve.tensor_copy(pool_a[:, WMAX:WMAX + 1], pool_u[:, 0:1]))
                if c == 0:
                    window(pool_b, pool_a, 2, upper)
                else:
                    window(pool_b, pool_a, 2)
                    window(pool_a, pool_b, 4)
                    window(pool_b, pool_a, 8, upper)
                counts = vec[:, V_COUNT + c * WMAX:V_COUNT + (c + 1) * WMAX]
                for rows, sums in ((slice(0, HD), pool_a), (upper, pool_b)):
                    dve.scalar_tensor_tensor(
                        out=pool_u[rows, WMAX:], in0=sums[rows, 2 * WMAX:],
                        scalar=counts[rows, WMAX - 1:WMAX], in1=pool_u[rows, WMAX:],
                        op0=ALU.mult, op1=ALU.subtract)
                    link(mul(sums[rows, WMAX:2 * WMAX], sums[rows, WMAX:2 * WMAX], counts[rows, :]))
                    last = dve.tensor_tensor(out=pool_u[rows, 0:WMAX],
                                             in0=sums[rows, WMAX:2 * WMAX],
                                             in1=pool_u[rows, 0:WMAX], op=ALU.subtract)
                last.then_inc(pooled_ready, 1)
                dve.wait_ge(pooled_hi, c + 1)
                lo_part(hid0[:, LO, c, :], pool_u, hid0[:, HI, c, :]).then_inc(pooled_split, 1)
                if c == 0:
                    dve.wait_ge(wp_hi, 1)
                    lo_part(wp_r[:, LO, :, :], wp_raw[:, :, :], wp_r[:, HI, :, :])\
                        .then_inc(wp_split, 1)

            dve.wait_ge(pooled_split, 2)
            link(dve.memset(conv_u[:, :, 0:TAPS - 1], 0.0))
            dve.wait_ge(proj_taken, done("cc1"))
            for c in range(2):
                name = "ch%d" % c
                u, y = conv_u[:, c, :], conv_cc[:, c, :]
                taken_and_linked(name, take(name, u[:, TAPS - 1:]))
                link(mul(u[:, TAPS - 1:], u[:, TAPS - 1:], y))
                tap = [vec[:, V_CONV + c * TAPS + w:V_CONV + c * TAPS + w + 1] for w in range(TAPS)]
                link(dve.tensor_scalar(y, u[:, TAPS - 1:], tap[TAPS - 1], None, ALU.mult))
                for w in range(TAPS - 1):
                    link(dve.scalar_tensor_tensor(out=y, in0=u[:, w:w + T], scalar=tap[w], in1=y,
                                                  op0=ALU.mult, op1=ALU.add))
            split_lo(w_o, 0, N_OUT_POOL)
            split_lo(w_b, 0, N_V0)
            for c in range(2):
                name = "cb%d" % c
                if c > 0:
                    dve.wait_ge(conv_y_ready, c)
                taken_and_linked(name, take(name, conv_b))
                mul(conv_cc[:, c, :], conv_cc[:, c, :], conv_b).then_inc(conv_y_ready, 1)

            for c in range(2):
                name = "pm%d" % c
                dve.wait_ge(pool_y_hi, c + 1)
                scaled_lo(hid0[:, LO, c, :], unit(SLOT[name]),
                          vec[:, V_PSCALE + c:V_PSCALE + c + 1], hid0[:, HI, c, :])\
                    .then_inc(proj_taken, 1)

            def values_of(n, name):
                dve.wait_ge(proj_ready, done(name))
                for i in range(4):
                    c = 4 * (n % 2) + i
                    last = dve.tensor_scalar(
                        v_plain[:, c, PAIR * (n // 2):PAIR * (n // 2 + 1)],
                        unit(SLOT[name])[:, i * PAIR:(i + 1) * PAIR], r_col[:, c:c + 1], None,
                        ALU.mult)
                last.then_inc(proj_taken, 1)

            split_lo(w_a, 0, N_V1)
            dve.wait_ge(conv_y_ready, 2)
            values_of(0, "v0a")
            values_of(1, "v0b")
            dve.wait_ge(wf_hi, 1)
            lo_part(wf[:, :, 32:32 + HEADS], wf_raw[:, :, :], wf[:, :, 0:HEADS])\
                .then_inc(wf_split, 1)
            for k in range(KD):
                now = X_MIX + k + 1
                residual(k, 1.0, now, now - KD, psum=unit(k % 4))
            for c in range(2):
                dve.wait_ge(conv_y_hi, c + 1)
                lo_part(hid0[:, LO, c, :], conv_cc[:, c, :], hid0[:, HI, c, :])\
                    .then_inc(conv_y_split, 1)
            split_lo(w_o, 0, N_OUT_CONV)
            values_of(2, "v1a")
            values_of(3, "v1b")
            split_lo(w_a, 0, N_Q0)

            def conv_share(k):
                now = X_MIX + KD + k + 1
                residual(k, 1.0, now, now - KD, psum=unit((3 + k) % 4))

            dve.wait_ge(forget_low, 1)
            add(row(1, 0), unit(SLOT["f"])[0:HEADS, :], row(0, 0)).then_inc(proj_taken, 1)
            conv_share(0)
            dve.wait_ge(proj_taken, done("f"))
            link(mul(row(1, 0), row(1, 0), r_rows[0:HEADS, :]))
            conv_share(1)
            link(dve.tensor_scalar(row(1, 0), row(1, 0), vec[0:HEADS, V_BFORGET:V_BFORGET + 1],
                                   None, ALU.add))
            dve.scalar_tensor_tensor(out=row(0, 0), in0=row(1, 0), scalar=-1.0, in1=row(1, 0),
                                     op0=ALU.mult, op1=ALU.max).then_inc(forget_abs, 1)
            conv_share(2)
            conv_share(3)
            split_lo(w_b, 0, N_Q1)
            conv_share(4)
            dve.wait_ge(forget_exp, 1)
            dve.tensor_scalar(row(1, 1), row(0, 1), 1.0, None, ALU.add).then_inc(forget_sum, 1)
            conv_share(5)
            conv_share(6)
            conv_share(7)
            dve.wait_ge(forget_log, 1)
            dve.scalar_tensor_tensor(out=row(1, 1), in0=row(1, 1), scalar=-1.0, in1=row(0, 1),
                                     op0=ALU.add, op1=ALU.subtract).then_inc(forget_lost, 1)
            dve.wait_ge(forget_inv, 1)
            link(mul(row(1, 2), row(1, 1), row(0, 1)))
            link(dve.tensor_tensor(out=row(0, 2), in0=row(0, 2), in1=row(1, 2), op=ALU.subtract))
            link(dve.tensor_scalar(row(1, 2), row(1, 0), -1.0, 0.0, ALU.mult, ALU.max))
            dve.tensor_tensor_scan(row(1, 0), row(1, 2), row(0, 2), 0.0, ALU.add, ALU.add)\
                .then_inc(decay_summed, 1)

            def rows_of(part, chunk):
                name = ("q%d" if part is q_plain else "k%d") % chunk
                take(name, part[:, chunk, :]).then_inc(proj_taken, 1)

            rows_of(q_plain, 0)
            rows_of(q_plain, 1)
            split_lo(w_a, 0, N_K0)
            rows_of(q_plain, 2)
            rows_of(q_plain, 3)
            split_lo(w_b, 0, N_K1)
            rows_of(k_plain, 0)
            rows_of(k_plain, 1)
            dve.memset(f32(decay_k[:, :]), 1.0)
            dve.memset(f32(decay_q[:, :]), 1.0).then_inc(decay_filled, 1)
            dve.wait_ge(decay_summed, 1)
            dve.wait_ge(decay_hi, 1)
            lo_part(decay_k[32:32 + HEADS, :], row(1, 0), decay_k[0:HEADS, :])\
                .then_inc(decay_lo, 1)
            rows_of(k_plain, 2)

            dve.wait_ge(mask_ready, 1)
            dve.wait_ge(decay_ready, 1)
            dve.tensor_scalar(decay_h[:, 0, :], f32(decay_k[:, :]), head_mask[:, 0:1], None,
                              ALU.mult).then_inc(decay_picked, 1)

            def keys(h, j):
                own, _ = halves(h % 2)
                dve.wait_ge(key_hi, heads_done(h, j))
                lo_part(k_lo[own, h % 2, :], of_pair(k_plain, own, h, j), k_hi[own, h % 2, :])\
                    .then_inc(key_lo, 1)

            def queries(h, j):
                own, other = halves(h % 2)
                dve.wait_ge(query_hi, heads_done(h, j))
                scaled_lo(q_st[other, h % 2, :], of_pair(q_plain, own, h, j), SCALE,
                          q_st[own, h % 2, :])\
                    .then_inc(query_split, 1)

            def values(h, j):
                dve.wait_ge(value_hi, heads_done(h, j))
                lo_part(v_st[:, h % 2, :, HD:2 * HD], v_of(h, j), v_st[:, h % 2, :, 0:HD])\
                    .then_inc(value_split, 1)

            def iteration(t, j):
                if 1 <= t < STEPS + 1:
                    r = t - 1
                    dve.wait_ge(exp_done, steps_done(r, j))
                    dve.reciprocal(exp_inv[:, r % NT:r % NT + 1], exp_sum[:, r % 2:r % 2 + 1])\
                        .then_inc(inverted, 1)
                if t < STEPS:
                    s, n = t % 2, P * (t % NT + 1)
                    dve.wait_ge(scores_ready, steps_done(t, j))
                    dve.tensor_reduce(minus_max[:, s:s + 1], unit(s)[:, 0:n], AX.X, ALU.max,
                                      negate=True).then_inc(max_ready, 1)
                if LAG <= t < STEPS + LAG:
                    r = t - LAG
                    to = P * (r % 2)
                    for bank, part in pt_banks(r):
                        dve.wait_ge(pt_hi, banks_done(r, j, bank))
                        lo_part(pt[r // 2 % 2][:, LO, part, to:to + P], chunks_in_psum(part),
                                pt[r // 2 % 2][:, HI, part, to:to + P]).then_inc(pt_split, 1)
                if t >= 5 and t % 2 == 1 and (t - 5) // 2 < STEPS // 2:
                    g = (t - 5) // 2
                    dve.wait_ge(y_low, groups_done(g, j))
                    add(y_of(g), ps[0:HD, 6 + g % 2, 0:QG], y_of(g)).then_inc(y_added, 1)
                    dve.wait_ge(y_added, groups_done(g, j))
                    mul(y_of(g), ps[0:HD, 6 + g % 2, QG:2 * QG], y_of(g)).then_inc(y_summed, 1)
                for offset, stage in ((4, keys), (5, queries), (NT + 2, values)):
                    h = blocks(t, offset)
                    if h is not None:
                        stage(h, j)
                if t >= TURN and t % TURN in Y_LO_AT:
                    pair, half = t // TURN - 1, Y_LO_AT.index(t % TURN)
                    cols = slice(half * BANK, (half + 1) * BANK)
                    at_pair = bass.ds(pair + j, 1)
                    dve.wait_ge(attn_y_hi, 2 * pair + half + 1 + 2 * j)
                    lo_part(y_lo[:, at_pair, cols].rearrange("p a t -> p (a t)"), y_f[:, cols],
                            y_hi[:, at_pair, cols].rearrange("p a t -> p (a t)"))\
                        .then_inc(attn_y_split, 1)
                if t == STEPS - 4:
                    split_lo(out_w[0], 0, N_OUT_A0)
                if t == STEPS - 3:
                    split_lo(out_w[1], 0, N_OUT_A1)

            queries(0, 0)
            dve.wait_ge(proj_ready, done("k3"))
            keys(0, 0)
            dve.wait_ge(proj_taken, done("k0"))
            lo_part(k_lo[HD:, 0, :], k_plain[0:HD, 0, :], k_hi[0:HD, 0, :])\
                .then_inc(key_stacked, 1)
            rows_of(k_plain, 3)
            pipeline(dve, iteration)

            split_lo(w_a, N_FFN[1], 0)
            gain_all(2, V_NORM2, lambda k: residual(k, 1.0, X_ATTN + k + 1, X_ATTN + k + 1 - KD,
                                                    psum=unit(k % 4)))
            split_lo(w_b, N_FFN[1], 1)
            other_squares(2)
            norm(2)

            def before_output(update):
                for k in range(KD + 1):
                    if k < KD:
                        update(k)
                    if k > 1:
                        sum_square(3, k - 1)
                inverse_rms(3)

            swiglu(1, before_output)
            dve.wait_ge(r_col_ready, 4)
            for c in range(0, NT, 2):
                dve.wait_ge(out_psum_ready, c + 1)
                dve.tensor_scalar(x_out[:, c, :], unit(c % 4), r_col[:, c:c + 1], None, ALU.mult)\
                    .then_inc(out_ready[0], 1)

        @block.tensor
        def _(pe):
            def projection(slot, w, chunk, ready, before=None, used_half=None):
                for k in range(KD):
                    if before:
                        before(k)
                    for half in range(2):
                        for a, b in PASSES:
                            last = pe.matmul(ps[:, 2 * slot + half, :],
                                             w[:, a, k, chunk * P:(chunk + 1) * P],
                                             xg[:, b, k, half * BANK:(half + 1) * BANK],
                                             start=(k == 0 and (a, b) == PASSES[0]),
                                             stop=(k == KD - 1 and (a, b) == PASSES[-1]))
                    if used_half and k == KD // 2 - 1:
                        last.then_inc(used_half, 1)
                last.then_inc(ready, 1)

            def behind_split(s):
                return lambda k: pe.wait_ge(xg_split, KD * (s + 1) + k + 1)

            def with_sums(s):
                return lambda k: sum_rows(s) if k == 2 else None

            def half_projection(bank, w, chunk, half, before=None):
                for k in range(KD):
                    if before:
                        before(k)
                    for a, b in PASSES:
                        last = pe.matmul(ps[:, bank, :], w[:, a, k, chunk * P:(chunk + 1) * P],
                                         xg[:, b, k, half * BANK:(half + 1) * BANK],
                                         start=(k == 0 and (a, b) == PASSES[0]),
                                         stop=(k == KD - 1 and (a, b) == PASSES[-1]))
                return last

            def output(bank, w, y, k, half):
                for f in range(2):
                    for a, b in PASSES:
                        last = pe.matmul(ps[:, bank, :], w[:, a, f, k * P:(k + 1) * P],
                                         y[:, b, f, half * BANK:(half + 1) * BANK],
                                         start=(f == 0 and (a, b) == PASSES[0]),
                                         stop=(f == 1 and (a, b) == PASSES[-1]))
                return last

            def sum_rows(s):
                pe.wait_ge(sumsq_added, (KD - 1) * s)
                for c in range(NT):
                    last = pe.matmul(ps[:, 2 * NORM_SLOT, 2 * c:2 * c + 2],
                                     tmp[:, 0, c * P:(c + 1) * P], ones2[:, :],
                                     start=True, stop=True)
                last.then_inc(r_sum_ready, 1)

            def spread_rows(s):
                pe.wait_ge(r_col_ready, s + 1)
                for c in range(NT):
                    last = pe.matmul(ps[:, 2 * NORM_SLOT + c // 4, c % 4 * P:(c % 4 + 1) * P],
                                     r_col[:, c:c + 1].to_broadcast([P, P]), ident[:, :],
                                     start=True, stop=True)
                last.then_inc(r_bcast_ready, 1)

            def swiglu(s):
                base, g0, x0 = N_FFN[s], 2 * GROUPS * s, X_BASE[s]

                def hidden(c, j):
                    i = counter(c, j)
                    for f in range(2):
                        if f == 0:
                            pe.wait_ge(weights_split, base + gate_pair(c) + 1 + 6 * j)
                        before = None
                        if c > 0:
                            pe.wait_ge(x_updated, i(KD, x0 - 2 * KD + 5 + 2 * f))
                            pe.wait_ge(gate_scaled, i(2, g0 + f - 1))
                        else:
                            pe.wait_ge(x_updated, x0 - 3 + 2 * f)
                            before = (behind_split(2 * s), with_sums(2 * s))[f]
                        projection(2 * f, w_a, f, gate_ready, before)
                        if c == 0 and f == 1:
                            spread_rows(2 * s)
                            pe.wait_ge(r_rows_ready, 2 * s + 1)
                        if f == 0:
                            pe.wait_ge(weights_split, base + gate_pair(c) + 2 + 6 * j)
                        if c > 0:
                            pe.wait_ge(x_updated, i(KD, x0 - 2 * KD + 6 + 2 * f))
                            pe.wait_ge(up_scaled, i(2, g0 + f - 1))
                        else:
                            pe.wait_ge(x_updated, x0 - 2 + 2 * f)
                        projection(2 * f + 1, w_b, f, up_ready)

                def down(c, j, last_group=False):
                    i = counter(c, j)
                    pe.wait_ge(weights_split, base + down_pair(c) + 1 + 6 * j)
                    pe.wait_ge(hidden_split, i(2, g0 + 2))
                    for k in range(KD):
                        if k >= 4 or last_group:
                            pe.wait_ge(x_updated, i(KD, x0 + k - 3))
                        else:
                            pe.wait_ge((gate_scaled, up_scaled)[k % 2], i(2, g0 + 3 + k // 2))
                        for half in range(2):
                            last = output(2 * (k % 4) + half, w_b_rows if last_group else w_o,
                                          hid[c % 2], k, half)
                        last.then_inc(x_psum_ready, 1)

                def first_hidden():
                    pe.wait_ge(weights_split, 1)
                    for half in range(2):
                        for f in range(2):
                            bank = 4 * f + half
                            pe.wait_ge(x_updated, KD + bank + 1)
                            last = half_projection(
                                bank, w_a, f, half,
                                lambda k: pe.wait_ge(xg_split, KD * half + k + 1))
                            if half == 1:
                                last.then_inc(gate_ready, 1)
                    pe.wait_ge(weights_split, 2)
                    pe.wait_ge(x_updated, KD + 4)
                    projection(1, w_b, 0, up_ready)
                    pe.wait_ge(x_updated, KD + 8)
                    spread_rows(0)
                    pe.wait_ge(r_rows_ready, 1)
                    projection(3, w_b, 1, up_ready)

                if s == 0:
                    first_hidden()
                else:
                    hidden(0, 0)
                with pe.Fori(0, TURNS) as j:
                    hidden(1, j)
                    down(0, j)
                    hidden(2, j)
                    down(1, j)
                down(GROUPS - 1, 0, True)

            pe.wait_ge(consts_ready, 1)
            for half in range(2):
                for c in range(2 * half, 2 * half + 2):
                    pe.wait_ge(x_loaded[c], 16)
                for k in range(KD):
                    if half == 1:
                        pe.wait_ge(x_updated, k + 1)
                    for c in range(4):
                        last = pe.transpose(ps[:, k, c * P:(c + 1) * P],
                                            x_in[:, 4 * half + c, k * P:(k + 1) * P], ident[:, :])
                    last.then_inc(x_psum_ready, 1)
            swiglu(0)

            pe.wait_ge(weights_split, N_POOL + 1)
            pe.wait_ge(x_updated, X_MIX - 3)
            projection(0, w_a, 0, proj_ready, behind_split(1))
            pe.wait_ge(x_updated, X_MIX - 2)
            projection(1, w_a, 1, proj_ready)
            pe.wait_ge(weights_split, N_CC + 1)
            pe.wait_ge(x_updated, X_MIX)
            projection(2, w_c, 0, proj_ready, with_sums(1))
            spread_rows(1)
            pe.wait_ge(r_rows_ready, 2)
            projection(3, w_c, 1, proj_ready)

            def pair(w, n, names, before):
                pe.wait_ge(weights_split, n + 1)
                for i, name in enumerate(names):
                    pe.wait_ge(proj_taken, done(before[i]))
                    projection(SLOT[name], w, i, proj_ready)

            pair(w_b, N_CH, ("ch0", "ch1"), ("pool0", "pool1"))
            pair(w_a, N_CB, ("cb0", "cb1"), ("cc0", "cc1"))
            pe.wait_ge(wp_split, 1)
            for c in range(2):
                pe.wait_ge(pooled_split, c + 1)
                pe.wait_ge(proj_taken, done("ch%d" % c))
                for half in range(2):
                    for a, b in PASSES:
                        last = pe.matmul(ps[:, 2 * SLOT["pm%d" % c] + half, :], wp_r[:, a, c, :],
                                         hid0[:, b, c, half * BANK:(half + 1) * BANK],
                                         start=(a, b) == PASSES[0], stop=(a, b) == PASSES[-1])
                last.then_inc(proj_ready, 1)

            def values_of(n, name):
                w = (w_b, w_a)[n // 2]
                pe.wait_ge(weights_split, (N_V0, N_V1)[n // 2] + 1)
                for i in range(4):
                    c = 4 * (n % 2) + i
                    for k in range(KD):
                        for a, b in PASSES:
                            last = pe.matmul(unit(SLOT[name])[:, i * PAIR:(i + 1) * PAIR],
                                             xg[:, b, k, c * P:(c + 1) * P], w[:, a, k, :],
                                             start=(k == 0 and (a, b) == PASSES[0]),
                                             stop=(k == KD - 1 and (a, b) == PASSES[-1]))
                last.then_inc(proj_ready, 1)

            def outputs(n, first_slot, x0, before):
                pe.wait_ge(weights_split, n + 1)
                for k in range(KD):
                    if k >= 4:
                        pe.wait_ge(x_updated, x0 + k - 3)
                    elif before[k] is None:
                        pe.wait_ge(x_updated, x0)
                    else:
                        pe.wait_ge(proj_taken, done(before[k]))
                    for half in range(2):
                        last = output(2 * ((first_slot + k) % 4) + half, w_o, hid0, k, half)
                    last.then_inc(x_psum_ready, 1)

            pe.wait_ge(proj_taken, done("cb0"))
            values_of(0, "v0a")
            pe.wait_ge(proj_taken, done("cb1"))
            values_of(1, "v0b")
            pe.wait_ge(proj_taken, done("pm1"))
            outputs(N_OUT_POOL, 0, X_MIX, ("pm0", "pm1", "v0a", "v0b"))
            pe.wait_ge(x_updated, X_MIX + KD - 3)
            values_of(2, "v1a")
            pe.wait_ge(x_updated, X_MIX + KD - 2)
            values_of(3, "v1b")
            pe.wait_ge(wf_split, 1)
            pe.wait_ge(x_updated, X_MIX + KD - 1)
            for half in range(2):
                for k in range(KD):
                    for b in (LO, HI):
                        last = pe.matmul(ps[:, 2 * SLOT["f"] + half, :], wf[:, k, :],
                                         xg[:, b, k, half * BANK:(half + 1) * BANK],
                                         start=(k == 0 and b == LO), stop=(k == KD - 1 and b == HI))
            last.then_inc(proj_ready, 1)
            pe.wait_ge(conv_y_split, 2)
            outputs(N_OUT_CONV, 3, X_MIX + KD, (None, "v1a", "v1b", "f"))
            for n, (w, pairs, names) in enumerate((
                    (w_a, N_Q0, ("q0", "q1")), (w_b, N_Q1, ("q2", "q3")),
                    (w_a, N_K0, ("k0", "k1")), (w_b, N_K1, ("k2", "k3")))):
                pe.wait_ge(weights_split, pairs + 1)
                for i, name in enumerate(names):
                    if n < 2:
                        pe.wait_ge(x_updated, X_MIX + 2 * KD - 3 + 2 * n + i)
                    else:
                        pe.wait_ge(proj_taken, done("q%d" % (2 * (n - 2) + i)))
                    projection(SLOT[name], w, i, proj_ready,
                               used_half=xg_half_used if name == "k3" else None)

            pe.wait_ge(consts_rounded, 1)
            pe.wait_ge(proj_taken, done("k2"))
            pe.wait_ge(key_doubled, 1)

            def attention_output(k, chunks):
                for half in range(2):
                    cols = slice(half * BANK, (half + 1) * BANK)
                    for q in chunks:
                        for a, b in PASSES:
                            last = pe.matmul(ps[:, 2 * (k % 4) + half, :],
                                             out_w[q // 2][:, a, q % 2, k * P:(k + 1) * P],
                                             (y_hi, y_lo)[b][:, q, cols],
                                             start=(q == 0 and (a, b) == PASSES[0]),
                                             stop=(q == 3 and (a, b) == PASSES[-1]))
                return last

            def scores(t, j):
                h, qb, s = t // NT, t % NT, t % 2
                b, n = h % 2, P * (qb + 1)
                if qb == 0:
                    pe.wait_ge(decay_picked, heads_done(h, j))
                    pe.wait_ge(query_split, heads_done(h, j))
                    pe.wait_ge(key_stacked, heads_done(h, j))
                if t >= 2:
                    pe.wait_ge(exp_done, steps_done(t - 2, j))
                queries = slice(qb * P, (qb + 1) * P)
                for bank in range((n + BANK - 1) // BANK):
                    keys = slice(bank * BANK, min(n, (bank + 1) * BANK))
                    diagonal = keys.stop == n
                    dst = unit(s)[:, keys]
                    pe.matmul(dst, q_st[:, b, queries], k_lo[:, b, keys],
                              start=True, stop=False)
                    pe.matmul(dst, q_st[:, b, queries], k_hi[:, b, keys],
                              start=False, stop=False)
                    pe.matmul(dst, decay_q[:, queries], decay_h[:, b, keys],
                              start=False, stop=not diagonal)
                pe.matmul(unit(s)[:, queries], ident_r[:, :], causal_r[:, :],
                          start=False, stop=True).then_inc(scores_ready, 1)

            def iteration(t, j):
                if LAG <= t < STEPS + LAG:
                    r = t - LAG
                    pe.wait_ge(exp_done, steps_done(r, j))
                    if r == 0:
                        pe.wait_ge(proj_taken, done("k3"))
                    for bank, part in pt_banks(r):
                        if r >= 1:
                            pe.wait_ge(pt_split, banks_done(r - 1, j, bank))
                        for c in range(part.start, part.stop):
                            last = pe.transpose(unit(2)[:, c * P:(c + 1) * P],
                                                prob[r % 2][:, c * P:(c + 1) * P], ident[:, :])
                        last.then_inc(transposed, 1)
                if t + 1 < STEPS:
                    scores(t + 1, j)
                if t >= 4 and t % 2 == 0 and (t - 4) // 2 < STEPS // 2:
                    g = (t - 4) // 2
                    b, q = g // HEAD_GROUPS % 2, g % HEAD_GROUPS
                    if q == 0:
                        pe.wait_ge(value_split, heads_done(g // HEAD_GROUPS, j))
                    pe.wait_ge(pt_split, banks_done(2 * g + 1, j))
                    if g >= 2:
                        pe.wait_ge(y_summed, groups_done(g - 2, j))
                    pe.wait_ge(inverted, steps_done(2 * g + 1, j))
                    for i in range(2):
                        r = (2 * g + i) % NT
                        pe.matmul(ps[0:HD, 6 + g % 2, QG + i * P:QG + (i + 1) * P],
                                  exp_inv[:, r:r + 1].to_broadcast([P, HD]), ident[:, :],
                                  start=True, stop=True)
                    chunks = 2 * q + 2
                    for c in range(chunks):
                        start = max(0, c * P - q * QG)
                        for part in (LO, HI):
                            last = pe.matmul(ps[:, 6 + g % 2, start:QG], v_st[:, b, c, :],
                                             pt[g % 2][:, part, c, start:QG],
                                             start=(c == 0 and part == LO),
                                             stop=(c == chunks - 1 and part == HI))
                    last.then_inc(pv_ready, 1)
                if t == STEPS + LAG - 1:
                    pe.wait_ge(weights_split, N_OUT_A1 + 1)
                    pe.wait_ge(attn_y_split, 6)
                    pe.wait_ge(exp_done, STEPS)
                    attention_output(0, range(3))
                if t == STEPS + LAG:
                    attention_output(1, range(3))
                    attention_output(2, range(3))

            scores(0, 0)
            pipeline(pe, iteration)
            pe.wait_ge(attn_y_split, 8)
            for k in range(KD):
                if k == 3:
                    pe.wait_ge(y_summed, STEPS // 2)
                if k >= 4:
                    pe.wait_ge(x_updated, X_ATTN + k - 3)
                attention_output(k, range(3, 4) if k < 3 else range(4)).then_inc(x_psum_ready, 1)

            swiglu(1)

            sum_rows(3)
            for c in range(NT):
                if c == 3:
                    pe.wait_ge(r_col_ready, 4)
                if c >= 4:
                    pe.wait_ge(out_ready[c % 2], c // 2 - 1)
                pe.wait_ge(gained, KD)
                for k in range(KD):
                    last = pe.transpose(unit(c % 4)[:, k * P:(k + 1) * P],
                                        x_gain[:, k, c * P:(c + 1) * P], ident[:, :])
                last.then_inc(out_psum_ready, 1)


def kernel(**inputs):
    import numpy as np
    import concourse.bacc as bacc
    from concourse.bass_utils import run_bass_kernel_spmd

    def chunked(a):
        return np.ascontiguousarray(np.asarray(a).reshape(-1, P).T)

    inv_counts = np.zeros((P, 2, WMAX), np.float32)
    for g, w in enumerate(WINDOWS):
        rows = slice((g % 2) * HD, (g % 2 + 1) * HD)
        inv_counts[rows, g // 2, :] = 1.0 / np.minimum(np.arange(WMAX) + 1, w)
    forget = np.zeros((P, 1), np.float32)
    forget[:HEADS, 0] = np.asarray(inputs["b_forget"])[0]
    taps = np.asarray(inputs["conv_w"])[0].reshape(TAPS, 2, P).transpose(2, 1, 0)
    vectors = np.concatenate(
        [chunked(inputs[n]) for n in ("norm_ffn1", "norm_mix", "norm_ffn2", "norm_final")]
        + [taps.reshape(P, 2 * TAPS), chunked(inputs["pool_scale"]), forget,
           inv_counts.reshape(P, 2 * WMAX)], axis=1)
    arrays = {
        "x": np.asarray(inputs["x"])[0],
        "w1_in": np.asarray(inputs["w_ffn1_in"])[0], "w1_out": np.asarray(inputs["w_ffn1_out"])[0],
        "wm_in": np.asarray(inputs["w_mix_in"])[0], "wm_out": np.asarray(inputs["w_mix_out"])[0],
        "w_pool": np.asarray(inputs["w_pool"])[0],
        "w2_in": np.asarray(inputs["w_ffn2_in"])[0], "w2_out": np.asarray(inputs["w_ffn2_out"])[0],
        "vectors": vectors,
    }
    nc = bacc.Bacc("TRN2", target_bir_lowering=False, num_devices=1)
    arrays = {"in_" + n: np.ascontiguousarray(a) for n, a in arrays.items()}
    args = [nc.dram_tensor(n, a.shape, mybir.dt.from_np(a.dtype), kind="ExternalInput").ap()
            for n, a in arrays.items()]
    out = nc.dram_tensor("out_x", (T, D), F32, kind="ExternalOutput").ap()
    trunk(nc, *args, out)
    result = run_bass_kernel_spmd(nc, [arrays], core_ids=[0])
    return result.results[0]["out_x"].reshape(1, T, D)
```
